# Optimizing a Trainium2 kernel written in Bass

```python
import jax, jax.numpy as jnp
from jax import lax
import numpy as np

D_MODEL = 1024
BATCH = 1
SEQ = 256
DEPTH = 2
DEC_BATCH = 1
DEC_SEQ = 32
PAST_LEN = 256

CHUNK = 64
N_MIXERS = 2
SB_HEADS = 16
SB_HEAD_DIM = D_MODEL // SB_HEADS
Q_BLOCK = 128
D_RNN = (4 * D_MODEL // 3) // 128 * 128
LRU_BLOCKS = 16
LRU_BLOCK = D_RNN // LRU_BLOCKS
CONV_W = 4
LRU_C = 8.0
D_FF = ((8 * D_MODEL // 3 + 255) // 256) * 256
PLE_DIM = 256
EPS = 1e-6

kernel_name = "stickbreak_rglru_macaron_stream_step"

def rmsnorm(x, g):
    xf = x.astype(jnp.float32)
    y = xf * lax.rsqrt(jnp.mean(xf * xf, axis=-1, keepdims=True) + EPS)
    return (y * g.astype(jnp.float32)).astype(x.dtype)

def swiglu(x, w_gate, w_up, w_down):
    return (jax.nn.silu(x @ w_gate) * (x @ w_up)) @ w_down

def sb_attend(q, k, v, q_pos, k_pos):
    z = jnp.einsum('bqhd,bkhd->bhqk', q.astype(jnp.float32), k.astype(jnp.float32)) * (SB_HEAD_DIM ** -0.5)
    mask = k_pos[None, :] < q_pos[:, None]
    log_stay = jnp.where(mask, jax.nn.log_sigmoid(-z), 0.0)
    after = lax.cumsum(log_stay, axis=3, reverse=True) - log_stay
    w = jnp.where(mask, jnp.exp(jax.nn.log_sigmoid(z) + after), 0.0)
    return jnp.einsum('bhqk,bkhd->bqhd', w, v.astype(jnp.float32)).astype(q.dtype)

def sb_qkv(xn, w_qkv):
    B, T, _ = xn.shape
    qkv = (xn @ w_qkv).reshape(B, T, 3, SB_HEADS, SB_HEAD_DIM)
    return qkv[:, :, 0], qkv[:, :, 1], qkv[:, :, 2]

def sb_mixer_prompt(xn, w_qkv, w_o):
    B, T, _ = xn.shape
    q, k, v = sb_qkv(xn, w_qkv)
    pos = jnp.arange(T)
    outs = []
    for b0 in range(0, T, Q_BLOCK):
        b1 = min(b0 + Q_BLOCK, T)
        outs.append(sb_attend(q[:, b0:b1], k[:, :b1], v[:, :b1], pos[b0:b1], pos[:b1]))
    o = jnp.concatenate(outs, axis=1).reshape(B, T, D_MODEL)
    return o @ w_o, k, v

def sb_mixer_sample(xn, cache_k, cache_v, w_qkv, w_o):
    B, T, _ = xn.shape
    P = cache_k.shape[1]
    q, k, v = sb_qkv(xn, w_qkv)
    k_all = jnp.concatenate([cache_k.astype(k.dtype), k], axis=1)
    v_all = jnp.concatenate([cache_v.astype(v.dtype), v], axis=1)
    o = sb_attend(q, k_all, v_all, P + jnp.arange(T), jnp.arange(P + T))
    return o.reshape(B, T, D_MODEL) @ w_o, k, v

def _lin_combine(e1, e2):
    a1, b1 = e1
    a2, b2 = e2
    return a1 * a2, a2 * b1 + b2

def lru_mixer(xn, h0, conv0, w_in, conv_w, conv_b, w_a, b_a, w_x, b_x, lam, w_o):
    B, T, _ = xn.shape
    gx = xn @ w_in
    gate = jax.nn.gelu(gx[..., :D_RNN])
    u = gx[..., D_RNN:]
    ext = jnp.concatenate([conv0.astype(u.dtype), u], axis=1)
    c = conv_b + sum(ext[:, j:j + T] * conv_w[j] for j in range(CONV_W))
    new_conv = ext[:, -(CONV_W - 1):]
    cb = c.reshape(B, T, LRU_BLOCKS, LRU_BLOCK)
    r = jax.nn.sigmoid(jnp.einsum('btnj,njk->btnk', cb, w_a).reshape(B, T, D_RNN) + b_a)
    gin = jax.nn.sigmoid(jnp.einsum('btnj,njk->btnk', cb, w_x).reshape(B, T, D_RNN) + b_x)
    log_a = (-LRU_C * jax.nn.softplus(-lam.astype(jnp.float32))) * r.astype(jnp.float32)
    a = jnp.exp(log_a)
    bterm = jnp.sqrt(-jnp.expm1(2.0 * log_a)) * (gin * c).astype(jnp.float32)
    bterm = bterm.at[:, 0].add(a[:, 0] * h0.astype(jnp.float32))
    _, h = lax.associative_scan(_lin_combine, (a, bterm), axis=1)
    y = (h.astype(xn.dtype) * gate) @ w_o
    return y, h[:, -1], new_conv

def layer_forward(x, p_i, norm_g, w1g, w1u, w1d, w2g, w2u, w2d, w_pe, w_pg, mix):
    x = x + 0.5 * swiglu(rmsnorm(x, norm_g[0]), w1g, w1u, w1d)
    y, st = mix(rmsnorm(x, norm_g[1]))
    x = x + y
    x = x + 0.5 * swiglu(rmsnorm(x, norm_g[2]), w2g, w2u, w2d)
    x = x + (p_i @ w_pe) * jax.nn.sigmoid(rmsnorm(x, norm_g[3]) @ w_pg)
    return x, st

def setup_inputs(seed: int = 0) -> dict:
    key = jax.random.key(seed)
    ks = jax.random.split(key, 32)
    n_sb = (DEPTH + 1) // 2
    n_lru = DEPTH // 2
    f32 = jnp.float32

    def nrm(k, shape, scale):
        return jax.random.normal(k, shape, f32) * scale

    u = jax.random.uniform(ks[25], (n_lru, D_RNN), f32, 0.9, 0.999)
    a_base = u ** (1.0 / LRU_C)
    lam = jnp.log(a_base) - jnp.log1p(-a_base)
    return {
        'x_prompt': nrm(ks[0], (BATCH, SEQ, D_MODEL), 1.0),
        'x_sample': nrm(ks[1], (DEC_BATCH, DEC_SEQ, D_MODEL), 1.0),
        'p_prompt': nrm(ks[2], (DEPTH, BATCH, SEQ, PLE_DIM), 1.0),
        'p_sample': nrm(ks[3], (DEPTH, DEC_BATCH, DEC_SEQ, PLE_DIM), 1.0),
        'cache_sb_k': nrm(ks[4], (n_sb, DEC_BATCH, PAST_LEN, SB_HEADS, SB_HEAD_DIM), 1.0),
        'cache_sb_v': nrm(ks[5], (n_sb, DEC_BATCH, PAST_LEN, SB_HEADS, SB_HEAD_DIM), 1.0),
        'state_lru_h': nrm(ks[6], (n_lru, DEC_BATCH, D_RNN), 0.5),
        'state_lru_conv': nrm(ks[7], (n_lru, DEC_BATCH, CONV_W - 1, D_RNN), 1.0),
        'norm_g': 1.0 + nrm(ks[8], (DEPTH, 4, D_MODEL), 0.02),
        'ffn_w_gate': nrm(ks[9], (DEPTH, 2, D_MODEL, D_FF), D_MODEL ** -0.5),
        'ffn_w_up': nrm(ks[10], (DEPTH, 2, D_MODEL, D_FF), D_MODEL ** -0.5),
        'ffn_w_down': nrm(ks[11], (DEPTH, 2, D_FF, D_MODEL), D_FF ** -0.5),
        'ple_w_proj': nrm(ks[12], (DEPTH, PLE_DIM, D_MODEL), PLE_DIM ** -0.5),
        'ple_w_gate': nrm(ks[13], (DEPTH, D_MODEL, D_MODEL), D_MODEL ** -0.5),
        'sb_w_qkv': nrm(ks[14], (n_sb, D_MODEL, 3 * D_MODEL), D_MODEL ** -0.5),
        'sb_w_o': nrm(ks[15], (n_sb, D_MODEL, D_MODEL), D_MODEL ** -0.5),
        'lru_w_in': nrm(ks[16], (n_lru, D_MODEL, 2 * D_RNN), D_MODEL ** -0.5),
        'lru_conv_w': nrm(ks[17], (n_lru, CONV_W, D_RNN), CONV_W ** -0.5),
        'lru_conv_b': nrm(ks[18], (n_lru, D_RNN), 0.01),
        'lru_w_a': nrm(ks[19], (n_lru, LRU_BLOCKS, LRU_BLOCK, LRU_BLOCK), LRU_BLOCK ** -0.5),
        'lru_b_a': nrm(ks[20], (n_lru, D_RNN), 0.01),
        'lru_w_x': nrm(ks[21], (n_lru, LRU_BLOCKS, LRU_BLOCK, LRU_BLOCK), LRU_BLOCK ** -0.5),
        'lru_b_x': nrm(ks[22], (n_lru, D_RNN), 0.01),
        'lru_lambda': lam,
        'lru_w_o': nrm(ks[23], (n_lru, D_RNN, D_MODEL), D_RNN ** -0.5),
        'final_norm_g': 1.0 + nrm(ks[24], (D_MODEL,), 0.02),
    }

def reference(x_prompt, x_sample, p_prompt, p_sample, cache_sb_k, cache_sb_v, state_lru_h, state_lru_conv,
              norm_g, ffn_w_gate, ffn_w_up, ffn_w_down, ple_w_proj, ple_w_gate, sb_w_qkv, sb_w_o,
              lru_w_in, lru_conv_w, lru_conv_b, lru_w_a, lru_b_a, lru_w_x, lru_b_x, lru_lambda, lru_w_o,
              final_norm_g):
    xp, xs = x_prompt, x_sample
    kp, vp, ks_, vs_ = [], [], [], []
    hp, cp, hs, cs = [], [], [], []
    for i in range(DEPTH):
        j = i // N_MIXERS
        if i % N_MIXERS == 0:
            wq, wo = sb_w_qkv[j], sb_w_o[j]
            ck, cv = cache_sb_k[j], cache_sb_v[j]
            mix_p = lambda xn, wq=wq, wo=wo: (lambda r: (r[0], (r[1], r[2])))(sb_mixer_prompt(xn, wq, wo))
            mix_s = lambda xn, wq=wq, wo=wo, ck=ck, cv=cv: (lambda r: (r[0], (r[1], r[2])))(sb_mixer_sample(xn, ck, cv, wq, wo))
        else:
            lw = (lru_w_in[j], lru_conv_w[j], lru_conv_b[j], lru_w_a[j], lru_b_a[j],
                  lru_w_x[j], lru_b_x[j], lru_lambda[j], lru_w_o[j])
            h0s, c0s = state_lru_h[j], state_lru_conv[j]
            mix_p = lambda xn, lw=lw: (lambda r: (r[0], (r[1], r[2])))(lru_mixer(
                xn, jnp.zeros((xn.shape[0], D_RNN), jnp.float32),
                jnp.zeros((xn.shape[0], CONV_W - 1, D_RNN), xn.dtype), *lw))
            mix_s = lambda xn, lw=lw, h0s=h0s, c0s=c0s: (lambda r: (r[0], (r[1], r[2])))(lru_mixer(xn, h0s, c0s, *lw))
        common = (norm_g[i], ffn_w_gate[i, 0], ffn_w_up[i, 0], ffn_w_down[i, 0],
                  ffn_w_gate[i, 1], ffn_w_up[i, 1], ffn_w_down[i, 1], ple_w_proj[i], ple_w_gate[i])
        xp, stp = layer_forward(xp, p_prompt[i], *common, mix_p)
        xs, sts = layer_forward(xs, p_sample[i], *common, mix_s)
        if i % N_MIXERS == 0:
            kp.append(stp[0]); vp.append(stp[1]); ks_.append(sts[0]); vs_.append(sts[1])
        else:
            hp.append(stp[0]); cp.append(stp[1]); hs.append(sts[0]); cs.append(sts[1])
    y_prompt = rmsnorm(xp, final_norm_g)
    y_sample = rmsnorm(xs, final_norm_g)
    return (y_prompt, y_sample,
            jnp.stack(kp), jnp.stack(vp), jnp.stack(hp), jnp.stack(cp),
            jnp.stack(ks_), jnp.stack(vs_), jnp.stack(hs), jnp.stack(cs))


_drawn_inputs = setup_inputs


def setup_inputs(seed=0):
    import zlib

    import numpy as np

    out = dict(_drawn_inputs(seed))
    spreads = {}
    factors = {'lru_b_a': 26.352, 'lru_b_x': 8.0, 'final_norm_g': 8.129}
    for name, (base, spread) in spreads.items():
        noise = np.random.default_rng([zlib.crc32(name.encode()), seed]).standard_normal(out[name].shape)
        drawn = base * np.exp(spread * noise) if base else spread * noise
        out[name] = __import__('jax').numpy.asarray(drawn.astype(out[name].dtype))
    for name, factor in factors.items():
        out[name] = (out[name] * factor).astype(out[name].dtype)
    return out
```

```python
from contextlib import ExitStack

import concourse.bass as bass
import numpy as np
from concourse import mybir

F32 = mybir.dt.float32
F32R = mybir.dt.float32r
ALU = mybir.AluOpType
ACT = mybir.ActivationFunctionType

P = 128
D_MODEL = 1024
D_FF = 2816
D_RNN = 1280
PLE_DIM = 256
HEADS = 16
HEAD_DIM = D_MODEL // HEADS
SEQ = 256
DEC = 32
PAST = 256
CONV_W = 4
LRU_BLOCKS = 16
LRU_C = 8.0
EPS = 1e-6

TOK = SEQ + DEC
KD = D_MODEL // P
KF = D_FF // P
KR = D_RNN // P
KP = PLE_DIM // P
PAIRS = HEADS // 2
HALO = CONV_W - 1
EXT = HALO + SEQ + HALO + DEC + 1
CW = EXT - HALO
SAMPLE = SEQ + HALO
HALF = KR // 2
LRU_BLOCK = D_RNN // LRU_BLOCKS
BAND = [[k for k in range(HALF)
         if any(b * LRU_BLOCK < (k + 1) * P and (b + 1) * LRU_BLOCK > k * P
                and b * LRU_BLOCK < (m + 1) * P and (b + 1) * LRU_BLOCK > m * P for b in range(LRU_BLOCKS // 2))]
        for m in range(HALF)]
STAGES = 9
SQUARES_BEFORE = [0] + [KD // 2 - 1 + n * (KD - 1) for n in range(STAGES - 1)]
BAND_TILES = sum(map(len, BAND))

C0, C1, NW, S1, S0, SCOLS = 0, DEC, 2 * DEC, 3 * DEC, 3 * DEC + P, 3 * DEC + P + SEQ
MASKED = slice(NW, S0 + P)

VECS = {"g": STAGES * KD, "conv_w": CONV_W * KR, "conv_b": KR, "b_a": KR, "b_x": KR, "lam": KR, "h0": KR}


class Phase:

    def __init__(self, name, stage, groups, tiles, body=2, head=0, counted=False):
        self.name, self.kind, self.stage, self.groups, self.tiles = name, name.rstrip("0123"), stage, groups, tiles
        self.body, self.head = body, head
        self.counted = counted
        self.part_a = (tiles + 1) // 2


def plan():
    def ffn(n, stage):
        return [Phase(f"up{n}", stage, KF, 2 * KD, head=2, counted=True),
                Phase(f"down{n}", stage, 2 * KD, KF // 2, body=4, head=4)]

    def ple(n, stage):
        return [Phase(f"ple{n}", stage, KD, KD + KP, head=2, counted=True)]

    phases = ffn(0, 0)
    phases += [Phase("qkv", 1, 3 * KD // 2, 2 * KD, head=2, counted=True), Phase("wo", 1, KD // 2, 2 * KD, body=4)]
    phases += ffn(1, 2) + ple(0, 3) + ffn(2, 4)
    phases += [Phase("lru_u", 5, KR, KD, head=2, counted=True), Phase("gates", 5, 4, BAND_TILES, body=4),
               Phase("lru_g", 5, KR, KD, body=KR, counted=True), Phase("lru_o", 5, KD, KR, head=2)]
    phases += ffn(3, 6) + ple(1, 7)
    group = pair = 0
    for p in phases:
        p.first_group, p.first_pair = group, pair
        group += p.groups
        pair += p.groups if p.counted else 0
    return phases


PHASES = plan()


def run_groups(eng, phase, step):
    for n in range(phase.head):
        step(None, n, n % phase.body)
    turns = (phase.groups - phase.head) // phase.body - 1
    if turns > 0:
        with eng.Fori(0, turns) as turn:
            for b in range(phase.body):
                step(turn, phase.head + b, b)
    for n in range(phase.groups - phase.body, phase.groups):
        step(None, n, n % phase.body)


def index(turn, n, per_turn):
    return n if turn is None else turn * per_turn + n


def one(i):
    return slice(i, i + 1) if isinstance(i, int) else bass.ts(i, 1)


def wait(eng, sem, value):
    if not isinstance(value, int) or value > 0:
        eng.wait_ge(sem, value)


def build(nc, a):
    ctx = ExitStack()
    with ctx:
        def sb(name, shape, dt=F32, scope=ctx):
            return scope.enter_context(nc.sbuf_tensor(name, shape, dt))

        def sem(name):
            return ctx.enter_context(nc.semaphore(name))

        bank = [ctx.enter_context(nc.psum_tensor(f"bank{i}", [P, 512], F32)) for i in range(8)]

        x = sb("x_res", [P, KD, TOK])
        xg_main = (sb("xg_hi", [P, KD, TOK], F32R), sb("xg_lo", [P, KD, TOK], F32R))
        raw = [sb(f"raw{i}", [P, 2 * KD * P]) for i in range(2)]
        w_hi = [sb(f"w_hi{i}", [P, 2 * KD * P], F32R) for i in range(2)]
        w_lo = [sb(f"w_lo{i}", [P, 2 * KD * P], F32R) for i in range(2)]
        vecs = sb("vecs_sb", [P, sum(VECS.values())])
        vec, at = {}, 0
        for n, w in VECS.items():
            vec[n] = vecs[:, at:at + w]
            at += w
        gain = vec["g"].rearrange("p (s k) -> p s k", s=STAGES)
        p_hi = sb("p_hi", [P, 2 * KP, TOK], F32R)
        p_lo = sb("p_lo", [P, 2 * KP, TOK], F32R)
        square = sb("square", [P, TOK])
        sum_squares = sb("sum_squares", [P, TOK])
        std = sb("std", [P, TOK])
        rstd = sb("rstd", [P, TOK])
        gate_in = sb("gate_in", [P, TOK])
        gate_act = sb("gate_act", [P, TOK])
        up_in = sb("up_in", [P, TOK])
        hidden = [sb(f"hidden{i}", [P, TOK]) for i in range(2)]
        mean_w = sb("mean_w", [P, P])
        eps_col = sb("eps_col", [P, 1])
        series = sb("series", [P, 7, KR])
        decay = sb("decay", [P, KR])

        with ExitStack() as scope:
            h_hi = sb("h_hi", [P, KF, TOK], F32R, scope)
            h_lo = sb("h_lo", [P, KF, TOK], F32R, scope)
            xg_side = (sb("xg_side_hi", [P, KD, TOK], F32R, scope), sb("xg_side_lo", [P, KD, TOK], F32R, scope))
            p_raw = sb("p_raw", [P, 2 * KP, TOK], F32, scope)
            first_squares = sb("first_squares", [P, KD // 2, TOK], F32, scope)
        with ExitStack() as scope:
            o_hi = sb("o_hi", [P, KD, TOK], F32R, scope)
            o_lo = sb("o_lo", [P, KD, TOK], F32R, scope)
            qkv = sb("qkv_sb", [P, 3 * KD, TOK], F32, scope)
            past_k = sb("past_k_sb", [P, PAIRS, PAST], F32, scope)
            past_v = sb("past_v_sb", [P, PAST // P, D_MODEL], F32, scope)
            k_now = [sb(f"k_now{i}", [P, TOK + PAST], F32, scope) for i in range(2)]
            q_now = [sb(f"q_now{i}", [P, TOK], F32, scope) for i in range(2)]
            v_now = [sb(f"v_now{i}", [P, 3 * P], F32, scope) for i in range(2)]
            pv_now = [sb(f"pv_now{i}", [P, PAST // P, P], F32, scope) for i in range(2)]
            v_rows = [sb(f"v_rows{i}", [P, 3 * P], F32, scope) for i in range(2)]
            log_part = [sb(f"log_part{i}", [P, SCOLS], F32, scope) for i in range(2)]
            stay = [sb(f"stay{i}", [P, SCOLS], F32, scope) for i in range(2)]
            log_sig = [sb(f"log_sig{i}", [P, SCOLS], F32, scope) for i in range(2)]
            weight = [sb(f"weight{i}", [P, SCOLS], F32, scope) for i in range(2)]
            mask = sb("mask", [P, SCOLS], F32, scope)
            later = sb("later", [P, P], F32, scope)
            ones = sb("ones", [P, P], F32, scope)
            ident = sb("ident", [P, P], F32, scope)
        with ExitStack() as scope:
            y_hi = sb("y_hi", [P, KR, TOK], F32R, scope)
            y_lo = sb("y_lo", [P, KR, TOK], F32R, scope)
            with ExitStack() as inner:
                c_hi = sb("c_hi", [P, KR, CW], F32R, inner)
                c_lo = sb("c_lo", [P, KR, CW], F32R, inner)
            gate_g = sb("gate_g", [P, KR, CW], F32, scope)
            h_g = sb("h_g", [P, KR, CW], F32, scope)
            u_ext = sb("u_ext", [P, KR, EXT], F32, scope)
            conv = sb("conv", [P, KR, CW], F32, scope)
            rate = sb("rate", [P, KR, CW], F32, scope)
            gated = sb("gated", [P, HALF, CW], F32, scope)
            a_square = sb("a_square", [P, HALF, CW], F32, scope)
            tails = sb("tails", [P, KR, 2 * HALO + 2], F32, scope)
        with ExitStack() as scope:
            y_rows = sb("y_rows", [P, KD, TOK], F32, scope)

        def xg_of(stage):
            return xg_side if stage == 4 else xg_main

        raw_landed = [sem("raw_landed0"), sem("raw_landed1")]
        raw_first = sem("raw_first")
        x_landed = [sem("x_landed0"), sem("x_landed1")]
        vecs_landed, p_landed = sem("vecs_landed"), sem("p_landed")
        past_landed, state_landed = sem("past_landed"), sem("state_landed")
        kv_stored, tails_stored = sem("kv_stored"), sem("tails_stored")
        y_stored = sem("y_stored")
        w_hi_done, w_lo_done = sem("w_hi_done"), sem("w_lo_done")
        tiles_done = sem("tiles_done")
        pair_free = sem("pair_free")
        x_new, xg_hi_done, xg_done = sem("x_new"), sem("xg_hi_done"), sem("xg_done")
        squared, summed_squares, first_squared = sem("squared"), sem("summed_squares"), sem("first_squared")
        consts, mean_done, std_done, rstd_done = sem("consts"), sem("mean_done"), sem("std_done"), sem("rstd_done")
        gate_in_done, gate_act_done = sem("gate_in_done"), sem("gate_act_done")
        hidden_done, hidden_hi_done, hidden_lo_done = sem("hidden_done"), sem("hidden_hi_done"), sem("hidden_lo_done")
        p_hi_done, p_done = sem("p_hi_done"), sem("p_done")
        decay_act, decay_dve = sem("decay_act"), sem("decay_dve")
        attn_consts = sem("attn_consts")
        kq_now_done, v_now_done = sem("kq_now_done"), sem("v_now_done")
        v_turned, v_rows_done = sem("v_turned"), sem("v_rows_done")
        scored, abs_done, exp_done, log_done = sem("scored"), sem("abs_done"), sem("exp_done"), sem("log_done")
        stay_done, log_sig_done, stay_masked = sem("stay_done"), sem("log_sig_done"), sem("stay_masked")
        later_summed, exponent_done = sem("later_summed"), sem("exponent_done")
        weight_done, weight_masked, mixed = sem("weight_done"), sem("weight_masked"), sem("mixed")
        o_hi_done, o_done = sem("o_hi_done"), sem("o_done")
        history_zero = sem("history_zero")
        conv_first, conv_step, c_hi_done, c_done = sem("conv_first"), sem("conv_step"), sem("c_hi_done"), sem("c_done")
        conv_tail = sem("conv_tail")
        gate_summed, gate_read = sem("gate_summed"), sem("gate_read")
        s_done, gated_used, tanh_done, a_done = sem("s_done"), sem("gated_used"), sem("tanh_done"), sem("a_done")
        a_square_done, b_square_done, b_root_done = sem("a_square_done"), sem("b_square_done"), sem("b_root_done")
        addend_done, h_done, gelu_done = sem("addend_done"), sem("h_done"), sem("gelu_done")
        y_prod, y_hi_done, y_done = sem("y_prod"), sem("y_hi_done"), sem("y_done")
        tails_done = sem("tails_done")
        out_ready = sem("out_ready")

        def group_dram(phase, i):
            kind, layer_ffn = phase.kind, phase.name[-1]
            if kind in ("up", "down"):
                return a[kind][one(int(layer_ffn) * phase.groups + i)] if isinstance(i, int) else \
                    a[kind][one(i + int(layer_ffn) * phase.groups)]
            if kind == "ple":
                return a[kind][one(i + int(layer_ffn) * phase.groups)]
            return a[phase.name][one(i)]

        block = ctx.enter_context(nc.Block())

        @block.sync
        def _(sp):
            sp.dma_start(vecs[:], a["vecs"]).then_inc(vecs_landed, 16)
            first = PHASES[0]
            parts = (slice(0, first.part_a * P), slice(first.part_a * P, first.tiles * P))
            for half in range(2):
                ks = slice(half * KD // 2, (half + 1) * KD // 2)
                sp.dma_start(x[:, ks, :], a["x"][:, ks, :]).then_inc(x_landed[half], 16)
                sp.dma_start(raw[0][:, parts[half]], group_dram(first, 0)[0, :, parts[half]]) \
                    .then_inc((raw_first, raw_landed[0])[half], 16)

            for phase in PHASES:
                def load(turn, n, b, phase=phase):
                    i = index(turn, n, phase.body)
                    if n == 0 and turn is None and phase is first:
                        return
                    wait(sp, w_lo_done, index(turn, 2 * (n + phase.first_group - 1), 2 * phase.body))
                    sp.dma_start(raw[b % 2][:, 0:phase.tiles * P],
                                 group_dram(phase, i).rearrange("a p c -> (a p) c")).then_inc(raw_landed[b % 2], 16)

                    if n == 1 and turn is None and phase is first:
                        sp.dma_start(p_raw[:], a["p"]).then_inc(p_landed, 16)

                run_groups(sp, phase, load)

            for k in range(KD):
                sp.wait_ge(out_ready, k + 1)
                sp.dma_start(a["y"][:, k, :], y_rows[:, k, :]).then_inc(y_stored, 16)
            sp.wait_ge(y_stored, 16 * KD)

        @block.gpsimd
        def _(pool):
            nc.gpsimd.memset(mean_w[:], 1.0 / D_MODEL).then_inc(consts, 1)
            nc.gpsimd.memset(eps_col[:], EPS).then_inc(consts, 1)

            def add_square(k, stage, term):
                nc.gpsimd.tensor_tensor(sum_squares[:], sum_squares[:], term, ALU.add).then_inc(summed_squares, 1)

            def square_of(k, stage):
                nc.gpsimd.tensor_tensor(square[:], x[:, k, :], x[:, k, :], ALU.mult).then_inc(squared, 1)
                pool.wait_ge(squared, k + SQUARES_BEFORE[stage])

            def squares(stage):
                pool.wait_ge(mean_done, stage)
                pool.wait_ge(x_new, (stage - 1) * KD + 1)
                nc.gpsimd.tensor_tensor(sum_squares[:], x[:, 0, :], x[:, 0, :], ALU.mult).then_inc(summed_squares, 1)
                with pool.Fori(1, KD) as k:
                    pool.wait_ge(x_new, k + ((stage - 1) * KD + 1))
                    pool.wait_ge(summed_squares, k + stage * KD)
                    square_of(k, stage)
                    add_square(k, stage, square[:])

            pool.wait_ge(x_landed[0], 16)
            nc.gpsimd.tensor_tensor(sum_squares[:], x[:, 0, :], x[:, 0, :], ALU.mult).then_inc(summed_squares, 1)
            for k in range(1, KD):
                pool.wait_ge(summed_squares, k)
                if k < KD // 2:
                    square_of(k, 0)
                elif k == KD // 2:
                    pool.wait_ge(first_squared, 1)
                add_square(k, 0, square[:] if k < KD // 2 else first_squares[:, k - KD // 2, :])
            squares(1)

            pool.wait_ge(x_new, KD)
            pool.dma_start(past_k[:], a["past_k"]).then_inc(past_landed, 16)
            pool.dma_start(past_v[:], a["past_v"]).then_inc(past_landed, 16)
            nc.gpsimd.memset(ones[:], 1.0).then_inc(attn_consts, 1)
            nc.gpsimd.memset(later[:], 1.0).then_inc(attn_consts, 1)
            nc.gpsimd.memset(ident[:], 0.0).then_inc(attn_consts, 1)
            nc.gpsimd.memset(mask[:], 1.0).then_inc(attn_consts, 1)
            for i in range(2):
                nc.gpsimd.memset(v_now[i][:], 0.0).then_inc(attn_consts, 1)
            pool.wait_ge(attn_consts, 6)
            nc.gpsimd.affine_select(out=later[:], in_=later[:], compare_op=ALU.is_gt, fill=0.0, base=0,
                                    pattern=[[-1, P]], channel_multiplier=1).then_inc(attn_consts, 1)
            nc.gpsimd.affine_select(out=ident[:], in_=ident[:], compare_op=ALU.not_equal, fill=1.0, base=0,
                                    pattern=[[-1, P]], channel_multiplier=1).then_inc(attn_consts, 1)
            for lo, n in ((S0, P), (S1, P), (NW, DEC)):
                nc.gpsimd.affine_select(out=mask[:, lo:lo + n], in_=mask[:, lo:lo + n], compare_op=ALU.is_gt,
                                        fill=0.0, base=0, pattern=[[1, n]], channel_multiplier=-1) \
                    .then_inc(attn_consts, 1)

            pool.wait_ge(attn_consts, 11)

            def attn_step(h, par):
                if h.has(2):
                    pool.wait_ge(stay_done, h(3))
                    nc.gpsimd.tensor_tensor(stay[par][:, MASKED], stay[par][:, MASKED], mask[:, MASKED], ALU.mult).then_inc(stay_masked, 1)
                if h.has(0):
                    pool.wait_ge(weight_done, h(1))
                    nc.gpsimd.tensor_tensor(weight[par][:, MASKED], weight[par][:, MASKED], mask[:, MASKED], ALU.mult) \
                        .then_inc(weight_masked, 1)

            attn_step(Head(None, -2), 0)
            attn_step(Head(None, -1), 1)
            qkv_phase = next(p for p in PHASES if p.name == "qkv")
            pool.wait_ge(pair_free, qkv_phase.first_pair + qkv_phase.groups)
            pool.dma_start(a["kv_new"], qkv[:, KD:3 * KD, :]).then_inc(kv_stored, 16)
            run_heads(pool, attn_step)

            for stage in range(2, 6):
                squares(stage)

            pool.wait_ge(x_new, 5 * KD)
            nc.gpsimd.memset(u_ext[:, :, 0:HALO], 0.0).then_inc(history_zero, 1)
            nc.gpsimd.memset(u_ext[:, :, EXT - 1:EXT], 0.0).then_inc(history_zero, 1)
            pool.dma_start(u_ext[:, :, SAMPLE:SAMPLE + HALO], a["conv_state"]).then_inc(state_landed, 16)

            with pool.Fori(0, KR) as m:
                pool.wait_ge(c_hi_done, m + 1)
                nc.gpsimd.tensor_tensor(c_lo[:, m, :], conv[:, m, :], c_hi[:, m, :].bitcast(F32), ALU.subtract) \
                    .then_inc(c_done, 1)

            pool.wait_ge(tails_done, 4)
            pool.dma_start(a["tails"], tails[:]).then_inc(tails_stored, 16)
            for stage in range(6, 9):
                squares(stage)
            pool.wait_ge(kv_stored, 16)
            pool.wait_ge(tails_stored, 16)

        @block.scalar
        def _(act):
            def w_split(target, part):
                phase, turn, n, b = target
                slot = b % 2
                loads = index(turn, phase.first_group // 2 + n // 2 + 1, phase.body // 2)
                cols = slice(0, phase.part_a * P) if part == 0 else slice(phase.part_a * P, phase.tiles * P)
                if phase is PHASES[0] and turn is None and n == 0:
                    act.wait_ge((raw_first, raw_landed[0])[part], 16)
                elif part == 0:
                    act.wait_ge(raw_landed[slot], loads * 16)
                    wait(act, tiles_done, index(turn, n + phase.first_group - 1, phase.body))
                nc.scalar.activation(w_hi[slot][:, cols], raw[slot][:, cols], ACT.Copy).then_inc(w_hi_done, 1)

            def xg_high(stage, k, from_x_new=True):
                if from_x_new:
                    act.wait_ge(x_new, k + ((stage - 1) * KD + 1))
                nc.scalar.activation(xg_of(stage)[0][:, k, :], x[:, k, :], ACT.Copy, scale=gain[:, stage, one(k)]) \
                    .then_inc(xg_hi_done, 1)

            def root(stage):
                act.wait_ge(mean_done, stage + 1)
                nc.scalar.activation(std[:], bank[7][:, 0:TOK], ACT.Sqrt, bias=eps_col[:]).then_inc(std_done, 1)

            nc.scalar.preload_act_table_set("silu_and_others")
            act.wait_ge(vecs_landed, 16)
            for half in range(2):
                act.wait_ge(x_landed[half], 16)
                for k in range(half * KD // 2, (half + 1) * KD // 2):
                    xg_high(0, k, from_x_new=False)
                w_split((PHASES[0], None, 0, 0), half)
            nc.scalar.activation(first_squares[:], x[:, KD // 2:KD, :], ACT.Square).then_inc(first_squared, 1)
            for part in range(2):
                w_split((PHASES[0], None, 1, 1), part)
            act.wait_ge(consts, 2)

            def attn_step(h, par):
                if h.has(2):
                    act.wait_ge(scored, h(3))
                    if not h.first(2):
                        act.wait_ge(log_sig_done, h(1))
                    nc.scalar.activation(log_part[par][:], bank[4 + par][:, 0:SCOLS], ACT.Abs).then_inc(abs_done, 1)
                    act.wait_ge(abs_done, h(3))
                    nc.scalar.activation(log_part[par][:], log_part[par][:], ACT.Exp, scale=-1.0).then_inc(exp_done, 1)
                    act.wait_ge(exp_done, h(3))
                    nc.scalar.activation(log_part[par][:], log_part[par][:], ACT.Ln, bias=1.0).then_inc(log_done, 1)
                if h.has(0):
                    act.wait_ge(exponent_done, h(1))
                    nc.scalar.activation(weight[par][:], weight[par][:], ACT.Exp).then_inc(weight_done, 1)
                if par == 0 and h.has(-2):
                    c = h.pair(-2)
                    act.wait_ge(mixed, h(0))
                    nc.scalar.activation(o_hi[:, c, :], bank[2 + h.pair_parity(-2)][:, 0:TOK], ACT.Copy) \
                        .then_inc(o_hi_done, 1)

            for at_phase, phase in enumerate(PHASES):
                after = PHASES[at_phase + 1] if at_phase + 1 < len(PHASES) else None
                stage, kind = phase.stage, phase.kind

                def step(turn, n, b, phase=phase, after=after, stage=stage, kind=kind):
                    i = index(turn, n, phase.body)
                    nxt = next_group(phase, after, turn, n, b)
                    if kind == "qkv" and turn is None and n >= phase.groups - 2:
                        if n == phase.groups - 2:
                            nc.scalar.preload_act_table_set("natural_log_exp_and_others")
                        attn_step(Head(None, n - phase.groups), n % 2)
                    if n == 0 and turn is None and kind in ("up", "qkv", "ple", "lru_u"):
                        root(stage)
                    if n == 0 and turn is None and phase.name == "up1":
                        act.wait_ge(kv_stored, 16)
                    if n == 0 and turn is None and phase.name == "up3":
                        act.wait_ge(tails_stored, 16)
                    if kind == "up":
                        part(nxt, 0)
                        act.wait_ge(gate_in_done, gate_base(phase) + 1 + i)
                        nc.scalar.activation(gate_act[:], gate_in[:], ACT.Silu).then_inc(gate_act_done, 1)
                        part(nxt, 1)
                        act.wait_ge(hidden_done, up_base(phase) + 1 + i)
                        nc.scalar.activation(h_hi[:, i, :], hidden[b % 2][:], ACT.Copy).then_inc(hidden_hi_done, 1)
                        if phase.name == "up0" and turn is None and n == 1:
                            act.wait_ge(p_landed, 16)
                            nc.scalar.activation(p_hi[:], p_raw[:], ACT.Copy).then_inc(p_hi_done, 1)
                    elif kind == "down":
                        if b % 2 == 1:
                            xg_high(stage + 1, index(turn, n // 2, phase.body // 2))
                        part(nxt, 0)
                        part(nxt, 1)
                    elif kind == "qkv":
                        part(nxt, 0)
                        part(nxt, 1)
                        if turn is None and n == 1:
                            nc.scalar.activation(series[:, 1, :], series[:, 0, :], ACT.Exp, scale=-1.0) \
                                .then_inc(decay_act, 1)
                    elif kind == "wo":
                        for o in range(2):
                            xg_high(stage + 1, 2 * n + o)
                        part(nxt, 0)
                        part(nxt, 1)
                    elif kind == "ple":
                        if turn is not None or n < phase.groups - 1:
                            part(nxt, 0)
                        act.wait_ge(gate_in_done, gate_base(phase) + 1 + i)
                        nc.scalar.activation(gate_act[:], gate_in[:], ACT.Sigmoid).then_inc(gate_act_done, 1)
                        if turn is not None or n < phase.groups - 1:
                            part(nxt, 1)
                        if stage + 1 < STAGES - 1:
                            xg_high(stage + 1, i)
                        if turn is None and n == phase.groups - 1:
                            part(nxt, 0)
                            part(nxt, 1)
                    elif kind == "lru_u":
                        part(nxt, 0)
                        act.wait_ge(pair_free, phase.first_pair + 1 + i)
                        if n == 0 and turn is None:
                            act.wait_ge(history_zero, 2)
                            act.wait_ge(state_landed, 16)
                        nc.scalar.activation(conv[:, i, :], u_ext[:, i, 0:CW], ACT.Identity,
                                             bias=vec["conv_b"][:, one(i)], scale=vec["conv_w"][:, one(i)]) \
                            .then_inc(conv_first, 1)
                        part(nxt, 1)
                        act.wait_ge(conv_step, i * HALO + HALO)
                        nc.scalar.activation(c_hi[:, i, :], conv[:, i, :], ACT.Copy).then_inc(c_hi_done, 1)
                    elif kind == "gates":
                        half, is_x = n // 2, n % 2
                        ms = slice(half * HALF, (half + 1) * HALF)
                        if n == 3:
                            act.wait_ge(gated_used, 1)
                        for m in range(HALF):
                            q = n * HALF + m
                            if m < HALF - 1:
                                act.wait_ge(gate_summed, n * (HALF - 1) + m + 1)
                            else:
                                act.wait_ge(tiles_done, phase.first_group + n + 1)
                            chunk = half * HALF + m
                            dst = gated[:, m, :] if is_x else rate[:, chunk, :]
                            bias = vec["b_x" if is_x else "b_a"][:, chunk:chunk + 1]
                            nc.scalar.activation(dst, bank[4 + q % 4][:, 0:CW], ACT.Sigmoid, bias=bias) \
                                .then_inc(gate_read, 1)
                        part(nxt, 0)
                        part(nxt, 1)
                        if is_x:
                            if half == 0:
                                act.wait_ge(conv_tail, 2)
                            act.wait_ge(s_done, half + 1)
                            nc.scalar.activation(u_ext[:, ms, 0:CW], rate[:, ms, :], ACT.Tanh).then_inc(tanh_done, 1)
                            act.wait_ge(tanh_done, half + 1)
                            nc.scalar.activation(rate[:, ms, :], rate[:, ms, :], ACT.Exp, scale=-1.0) \
                                .then_inc(a_done, 1)
                            act.wait_ge(a_done, half + 1)
                            if half == 1:
                                act.wait_ge(b_square_done, 1)
                            nc.scalar.activation(a_square[:], rate[:, ms, :], ACT.Square).then_inc(a_square_done, 1)
                        if n == 3:
                            b_root(0)
                    elif kind == "lru_g":
                        part(nxt, 0)
                        part(nxt, 1)
                        if n == 1:
                            b_root(1)
                        if n == HALF:
                            gelu(phase, 0)
                        if n >= HALF:
                            y_high(n - HALF)
                        if n == KR - 1:
                            gelu(phase, 1)
                            for m in range(HALF, KR):
                                y_high(m)
                    elif kind == "lru_o":
                        xg_high(stage + 1, i)
                        part(nxt, 0)
                        part(nxt, 1)

                def part(nxt, which):
                    if nxt is not None:
                        w_split(nxt, which)

                def b_root(half):
                    ms = slice(half * HALF, (half + 1) * HALF)
                    act.wait_ge(b_square_done, half + 1)
                    nc.scalar.activation(u_ext[:, ms, 0:CW], u_ext[:, ms, 0:CW], ACT.Sqrt).then_inc(b_root_done, 1)

                def gelu(phase, half):
                    ms = slice(half * HALF, (half + 1) * HALF)
                    act.wait_ge(pair_free, phase.first_pair + (half + 1) * HALF)
                    nc.scalar.activation(gate_g[:, ms, 0:TOK], gate_g[:, ms, 0:TOK], ACT.Gelu_apprx_tanh) \
                        .then_inc(gelu_done, 1)

                def y_high(m):
                    act.wait_ge(y_prod, m + 1)
                    nc.scalar.activation(y_hi[:, m, :], hidden[m % 2][:], ACT.Copy).then_inc(y_hi_done, 1)

                run_groups(act, phase, step)

                if phase.name == "up0":
                    nc.scalar.activation(series[:, 0, :], vec["lam"], ACT.Abs).then_inc(decay_act, 1)
                    act.wait_ge(decay_act, 1)
                if phase.name == "qkv":
                    run_heads(act, attn_step)
            root(STAGES - 1)

        @block.vector
        def _(dve):
            def w_split(target, which):
                phase, turn, n, b = target
                slot = b % 2
                cols = slice(0, phase.part_a * P) if which == 0 else slice(phase.part_a * P, phase.tiles * P)
                dve.wait_ge(w_hi_done, index(turn, 2 * (n + phase.first_group) + 1 + which, 2 * phase.body))
                nc.vector.tensor_tensor(w_lo[slot][:, cols], raw[slot][:, cols], w_hi[slot][:, cols].bitcast(F32),
                                        ALU.subtract).then_inc(w_lo_done, 1)

            def part(nxt, which):
                if nxt is not None:
                    w_split(nxt, which)

            def low_part(dst, src, hi, scalar, done):
                nc.vector.scalar_tensor_tensor(out=dst, in0=src, scalar=scalar, in1=hi.bitcast(F32), op0=ALU.mult,
                                               op1=ALU.subtract).then_inc(done, 1)

            def xg_low(stage, k):
                hi, lo = xg_of(stage)
                dve.wait_ge(xg_hi_done, k + (stage * KD + 1))
                low_part(lo[:, k, :], x[:, k, :], hi[:, k, :], gain[:, stage, one(k)], xg_done)

            def inverse(stage):
                dve.wait_ge(std_done, stage + 1)
                nc.vector.reciprocal(rstd[:], std[:]).then_inc(rstd_done, 1)
                dve.wait_ge(rstd_done, stage + 1)

            def add_to_x(k, product, factor):
                nc.vector.scalar_tensor_tensor(out=x[:, k, :], in0=product, scalar=factor, in1=x[:, k, :],
                                               op0=ALU.mult, op1=ALU.add).then_inc(x_new, 1)

            dve.wait_ge(vecs_landed, 16)
            for half in range(2):
                for k in range(half * KD // 2, (half + 1) * KD // 2):
                    xg_low(0, k)
                w_split((PHASES[0], None, 0, 0), half)
            for which in range(2):
                w_split((PHASES[0], None, 1, 1), which)

            def stage_kq(pair, slot):
                nc.vector.tensor_scalar(q_now[slot][:], qkv[:, pair, :], HEAD_DIM ** -0.5, None, ALU.mult)
                nc.vector.tensor_copy(k_now[slot][:, 0:TOK], qkv[:, pair + KD, :])
                nc.vector.tensor_copy(k_now[slot][:, TOK:TOK + PAST], past_k[:, pair, :]).then_inc(kq_now_done, 1)

            def stage_v(pair, slot):
                nc.vector.tensor_copy(v_now[slot][:, 0:TOK], qkv[:, pair + 2 * KD, :])
                nc.vector.tensor_copy(pv_now[slot][:], past_v[:, :, bass.ts(pair, P)]).then_inc(v_now_done, 1)

            def attn_step(h, par):
                if par == 0 and h.has(0):
                    slot = h.pair_parity(0)
                    dve.wait_ge(v_turned, h.pair_count(0, 1))
                    nc.vector.tensor_copy(v_rows[slot][:], bank[0][:, 0:3 * P]).then_inc(v_rows_done, 1)
                if par == 1 and h.has(3):
                    stage_kq(h.pair(3), h.pair_parity(3))
                if h.has(0):
                    dve.wait_ge(later_summed, h(1))
                    if not h.first(0):
                        dve.wait_ge(mixed, h(-1))
                    nc.vector.tensor_tensor(weight[par][:], log_sig[par][:], bank[6 + par][:, 0:SCOLS], ALU.subtract) \
                        .then_inc(exponent_done, 1)
                if h.has(2):
                    dve.wait_ge(log_done, h(3))
                    if not h.first(2):
                        dve.wait_ge(later_summed, h(1))
                    scores = bank[4 + par][:, 0:SCOLS]
                    nc.vector.scalar_tensor_tensor(out=stay[par][:], in0=scores, scalar=0.0, in1=log_part[par][:],
                                                   op0=ALU.max, op1=ALU.add).then_inc(stay_done, 1)
                    if not h.first(2):
                        dve.wait_ge(exponent_done, h(1))
                    nc.vector.scalar_tensor_tensor(out=log_sig[par][:], in0=scores, scalar=0.0, in1=log_part[par][:],
                                                   op0=ALU.min, op1=ALU.subtract).then_inc(log_sig_done, 1)
                if par == 0 and h.has(-2):
                    c = h.pair(-2)
                    dve.wait_ge(o_hi_done, h.pair_count(-2, 1))
                    nc.vector.tensor_tensor(o_lo[:, c, :], bank[2 + h.pair_parity(-2)][:, 0:TOK],
                                            o_hi[:, c, :].bitcast(F32), ALU.subtract).then_inc(o_done, 1)
                if par == 1 and h.has(1):
                    stage_v(h.pair(1), h.pair_parity(1))

            def decay_rates():
                steps = [0]

                def link(ins):
                    steps[0] += 1
                    ins.then_inc(decay_dve, 1)
                    dve.wait_ge(decay_dve, steps[0])

                dve.wait_ge(decay_act, 2)
                e, t, z, z2, poly = (series[:, n, :] for n in (1, 2, 3, 4, 5))
                link(nc.vector.tensor_scalar(t, e, 2.0, None, ALU.add))
                link(nc.vector.reciprocal(t, t))
                link(nc.vector.tensor_tensor(z, e, t, ALU.mult))
                link(nc.vector.tensor_tensor(z2, z, z, ALU.mult))
                link(nc.vector.tensor_scalar(poly, z2, 1.0 / 17, 1.0 / 15, ALU.mult, ALU.add))
                for n in (13, 11, 9, 7, 5, 3, 1):
                    link(nc.vector.tensor_tensor(poly, poly, z2, ALU.mult))
                    link(nc.vector.tensor_scalar(poly, poly, 1.0 / n, None, ALU.add))
                link(nc.vector.tensor_tensor(poly, poly, z, ALU.mult))
                link(nc.vector.tensor_scalar(t, vec["lam"], -1.0, 0.0, ALU.mult, ALU.max))
                link(nc.vector.scalar_tensor_tensor(out=t, in0=poly, scalar=2.0, in1=t, op0=ALU.mult, op1=ALU.add))
                link(nc.vector.tensor_scalar(decay[:], t, LRU_C, None, ALU.mult))

            def y_product(m):
                dve.wait_ge(gelu_done, m // HALF + 1)
                if m >= 2:
                    dve.wait_ge(y_done, m - 1)
                nc.vector.tensor_tensor(hidden[m % 2][:], h_g[:, m, 0:TOK], gate_g[:, m, 0:TOK], ALU.mult) \
                    .then_inc(y_prod, 1)

            def y_low(m):
                dve.wait_ge(y_hi_done, m + 1)
                nc.vector.tensor_tensor(y_lo[:, m, :], hidden[m % 2][:], y_hi[:, m, :].bitcast(F32), ALU.subtract) \
                    .then_inc(y_done, 1)

            def scan(m):
                dve.wait_ge(addend_done, m // HALF + 1)
                nc.vector.tensor_tensor_scan(h_g[:, m, 0:SEQ], rate[:, m, 0:SEQ], conv[:, m, 0:SEQ], 0.0,
                                             ALU.mult, ALU.add)
                nc.vector.tensor_tensor_scan(h_g[:, m, SEQ:TOK], rate[:, m, SAMPLE:SAMPLE + DEC], conv[:, m, SAMPLE:SAMPLE + DEC],
                                             vec["h0"][:, m:m + 1], ALU.mult, ALU.add).then_inc(h_done, 1)

            def b_square(half):
                ms = slice(half * HALF, (half + 1) * HALF)
                dve.wait_ge(a_square_done, half + 1)
                nc.vector.scalar_tensor_tensor(out=u_ext[:, ms, 0:CW], in0=a_square[:], scalar=1.0,
                                               in1=u_ext[:, ms, 0:CW], op0=ALU.add, op1=ALU.mult) \
                    .then_inc(b_square_done, 1)

            def addend(half):
                ms = slice(half * HALF, (half + 1) * HALF)
                dve.wait_ge(b_root_done, half + 1)
                dve.wait_ge(gated_used, half + 1)
                nc.vector.tensor_tensor(conv[:, ms, :], conv[:, ms, :], u_ext[:, ms, 0:CW], ALU.mult) \
                    .then_inc(addend_done, 1)

            for at_phase, phase in enumerate(PHASES):
                after = PHASES[at_phase + 1] if at_phase + 1 < len(PHASES) else None
                stage, kind = phase.stage, phase.kind

                def step(turn, n, b, phase=phase, after=after, stage=stage, kind=kind):
                    i = index(turn, n, phase.body)
                    nxt = next_group(phase, after, turn, n, b)
                    if kind == "qkv" and turn is None and n >= phase.groups - 2:
                        if n == phase.groups - 2:
                            dve.wait_ge(pair_free, phase.first_pair + n)
                            dve.wait_ge(past_landed, 32)
                            dve.wait_ge(attn_consts, 11)
                            stage_kq(0, 0)
                        attn_step(Head(None, n - phase.groups), n % 2)
                    if n == 0 and turn is None and kind in ("up", "qkv", "ple", "lru_u"):
                        inverse(stage)
                    if n == 0 and turn is None and phase.name == "up1":
                        dve.wait_ge(kv_stored, 16)
                    if n == 0 and turn is None and phase.name == "up3":
                        dve.wait_ge(tails_stored, 16)
                    first, second = (bank[b % 2 * 2 + o][:, 0:TOK] for o in range(2))
                    if kind != "gates" and not (kind == "down" and b % 2 == 0):
                        dve.wait_ge(tiles_done, phase.first_group + 1 + i)
                    if kind == "up":
                        nc.vector.tensor_tensor(gate_in[:], first, rstd[:], ALU.mult).then_inc(gate_in_done, 1)
                        nc.vector.tensor_tensor(up_in[:], second, rstd[:], ALU.mult).then_inc(pair_free, 1)
                        part(nxt, 0)
                        dve.wait_ge(gate_act_done, gate_base(phase) + 1 + i)
                        dve.wait_ge(pair_free, phase.first_pair + 1 + i)
                        nc.vector.tensor_tensor(hidden[b % 2][:], gate_act[:], up_in[:], ALU.mult) \
                            .then_inc(hidden_done, 1)
                        part(nxt, 1)
                        dve.wait_ge(hidden_hi_done, up_base(phase) + 1 + i)
                        nc.vector.tensor_tensor(h_lo[:, i, :], hidden[b % 2][:], h_hi[:, i, :].bitcast(F32),
                                                ALU.subtract).then_inc(hidden_lo_done, 1)
                        if phase.name == "up0" and turn is None and n == 1:
                            dve.wait_ge(p_hi_done, 1)
                            nc.vector.tensor_tensor(p_lo[:], p_raw[:], p_hi[:].bitcast(F32), ALU.subtract) \
                                .then_inc(p_done, 1)
                    elif kind == "down":
                        if b % 2 == 1:
                            j = index(turn, n // 2, phase.body // 2)
                            add_to_x(j, bank[4 + b // 2][:, 0:TOK], 0.5)
                            xg_low(stage + 1, j)
                        part(nxt, 0)
                        part(nxt, 1)
                    elif kind == "qkv":
                        nc.vector.tensor_tensor(qkv[:, i * 2, :], first, rstd[:], ALU.mult)
                        nc.vector.tensor_tensor(qkv[:, i * 2 + 1, :], second, rstd[:], ALU.mult).then_inc(pair_free, 1)
                        part(nxt, 0)
                        part(nxt, 1)
                        if turn is None and n == 1:
                            decay_rates()
                    elif kind == "wo":
                        for o, product in enumerate((first, second)):
                            add_to_x(2 * n + o, product, 1.0)
                        for o in range(2):
                            xg_low(stage + 1, 2 * n + o)
                        part(nxt, 0)
                        part(nxt, 1)
                    elif kind == "ple":
                        nc.vector.tensor_tensor(gate_in[:], first, rstd[:], ALU.mult).then_inc(gate_in_done, 1)
                        if turn is not None or n < phase.groups - 1:
                            part(nxt, 0)
                        dve.wait_ge(gate_act_done, gate_base(phase) + 1 + i)
                        nc.vector.tensor_tensor(hidden[b % 2][:], gate_act[:], second, ALU.mult).then_inc(pair_free, 1)
                        dve.wait_ge(pair_free, phase.first_pair + 1 + i)
                        add_to_x(i, hidden[b % 2][:], 1.0)
                        if turn is not None or n < phase.groups - 1:
                            part(nxt, 1)
                        if stage + 1 < STAGES - 1:
                            xg_low(stage + 1, i)
                        if turn is None and n == phase.groups - 1:
                            part(nxt, 0)
                            part(nxt, 1)
                    elif kind == "lru_u":
                        nc.vector.tensor_tensor(u_ext[:, i, HALO:HALO + SEQ], first[:, 0:SEQ], rstd[:, 0:SEQ], ALU.mult)
                        nc.vector.tensor_tensor(u_ext[:, i, SAMPLE + HALO:EXT - 1], first[:, SEQ:TOK], rstd[:, SEQ:TOK],
                                                ALU.mult).then_inc(pair_free, 1)
                        part(nxt, 0)
                        dve.wait_ge(conv_first, i + 1)
                        for tap in range(1, CONV_W):
                            if tap > 1:
                                dve.wait_ge(conv_step, i * HALO + (tap - 1))
                            w = vec["conv_w"][:, tap * KR:(tap + 1) * KR]
                            nc.vector.scalar_tensor_tensor(out=conv[:, i, :], in0=u_ext[:, i, tap:tap + CW],
                                                           scalar=w[:, one(i)], in1=conv[:, i, :],
                                                           op0=ALU.mult, op1=ALU.add).then_inc(conv_step, 1)
                        part(nxt, 1)
                    elif kind == "gates":
                        half, is_x = n // 2, n % 2
                        ms = slice(half * HALF, (half + 1) * HALF)
                        if n == 0:
                            nc.vector.tensor_copy(tails[:, :, 0:HALO], u_ext[:, :, SEQ:SEQ + HALO]).then_inc(conv_tail, 1)
                            nc.vector.tensor_copy(tails[:, :, HALO:2 * HALO], u_ext[:, :, SAMPLE + DEC:EXT - 1]) \
                                .then_inc(conv_tail, 1)
                        dve.wait_ge(gate_read, (n + 1) * HALF)
                        if is_x:
                            nc.vector.tensor_tensor(conv[:, ms, :], gated[:], conv[:, ms, :], ALU.mult) \
                                .then_inc(gated_used, 1)
                        else:
                            for m in range(half * HALF, (half + 1) * HALF):
                                s = nc.vector.tensor_scalar(rate[:, m, :], rate[:, m, :], decay[:, m:m + 1], None,
                                                            ALU.mult)
                            s.then_inc(s_done, 1)
                        part(nxt, 0)
                        part(nxt, 1)
                        if n == 2:
                            b_square(0)
                    elif kind == "lru_g":
                        nc.vector.tensor_tensor(gate_g[:, n, 0:TOK], first, rstd[:], ALU.mult).then_inc(pair_free, 1)
                        part(nxt, 0)
                        part(nxt, 1)
                        if n == 0:
                            b_square(1)
                            addend(0)
                        if n == 2:
                            addend(1)
                        if 1 <= n <= HALF:
                            scan(2 * n - 2)
                            scan(2 * n - 1)
                        if n >= HALF:
                            if n == HALF:
                                dve.wait_ge(h_done, KR)
                            y_product(n - HALF)
                            y_low(n - HALF)
                        if n == KR - 1:
                            for m in range(HALF, KR):
                                y_product(m)
                                if m > HALF:
                                    y_low(m - 1)
                            y_low(KR - 1)
                            nc.vector.tensor_copy(tails[:, :, 2 * HALO:2 * HALO + 1], h_g[:, :, SEQ - 1:SEQ]) \
                                .then_inc(tails_done, 2)
                            nc.vector.tensor_copy(tails[:, :, 2 * HALO + 1:2 * HALO + 2], h_g[:, :, TOK - 1:TOK]) \
                                .then_inc(tails_done, 2)
                    elif kind == "lru_o":
                        add_to_x(i, first, 1.0)
                        xg_low(stage + 1, i)
                        part(nxt, 0)
                        part(nxt, 1)

                run_groups(dve, phase, step)

                if phase.name == "qkv":
                    dve.wait_ge(pair_free, phase.first_pair + phase.groups)
                    run_heads(dve, attn_step)

            inverse(STAGES - 1)
            dve.wait_ge(x_new, (STAGES - 1) * KD)
            for k in range(KD):
                nc.vector.scalar_tensor_tensor(out=y_rows[:, k, :], in0=x[:, k, :], scalar=gain[:, STAGES - 1, k:k + 1],
                                               in1=rstd[:], op0=ALU.mult, op1=ALU.mult).then_inc(out_ready, 1)

        @block.tensor
        def _(pe):
            def product(out, slot, tile, operand, k, width, start, stop):
                hi, lo = operand
                cols = slice(tile * P, (tile + 1) * P)
                nc.tensor.matmul(out, w_hi[slot][:, cols], hi[:, k, 0:width], start=start, stop=False)
                nc.tensor.matmul(out, w_hi[slot][:, cols], lo[:, k, 0:width], start=False, stop=False)
                return nc.tensor.matmul(out, w_lo[slot][:, cols], hi[:, k, 0:width], start=False, stop=stop)

            def mean(stage):
                pe.wait_ge(summed_squares, (stage + 1) * KD)
                pe.wait_ge(consts, 2)
                nc.tensor.matmul(bank[7][:, 0:TOK], mean_w[:], sum_squares[:], start=True, stop=True) \
                    .then_inc(mean_done, 1)

            def attn_step(h, par):
                rows = slice(par * HEAD_DIM, (par + 1) * HEAD_DIM)
                if h.has(2):
                    slot = h.pair_parity(2 - par)
                    pe.wait_ge(kq_now_done, h.pair_count(2 - par, 1))
                    if not h.first(2):
                        pe.wait_ge(log_sig_done, h(1))
                    out, k, q = bank[4 + par], k_now[slot], q_now[slot]
                    for at, width, key, query in ((S0, SEQ, 0, 0), (S1, P, P, P), (C0, DEC, TOK, SEQ),
                                                  (C1, DEC, TOK + P, SEQ), (NW, DEC, SEQ, SEQ)):
                        last = nc.tensor.matmul(out[:, at:at + width], k[rows, key:key + P],
                                                q[rows, query:query + width], start=True, stop=True)
                    last.then_inc(scored, 1)
                if par == 0 and h.has(0):
                    slot = h.pair_parity(0)
                    pe.wait_ge(v_now_done, h.pair_count(0, 1))
                    if not h.first(0):
                        pe.wait_ge(v_rows_done, h.pair_count(0, 0))
                    for c in range(3):
                        last = nc.tensor.transpose(bank[0][:, c * P:(c + 1) * P], v_now[slot][:, c * P:(c + 1) * P],
                                                   ident[:])
                    last.then_inc(v_turned, 1)
                if h.has(0):
                    pe.wait_ge(stay_masked, h(1))
                    if not h.first(0):
                        pe.wait_ge(exponent_done, h(-1))
                    out, s = bank[6 + par], stay[par]
                    nc.tensor.matmul(out[:, 0:SCOLS], later[:], s[:, 0:SCOLS], start=True, stop=False)
                    nc.tensor.matmul(out[:, S0 + P:S0 + SEQ], ones[:], s[:, S1:S1 + P], start=False, stop=False)
                    nc.tensor.matmul(out[:, C0:NW], ones[:], s[:, C1:S1], start=False, stop=False)
                    nc.tensor.matmul(out[:, C0:C1], ones[:], s[:, NW:S1], start=False, stop=True) \
                        .then_inc(later_summed, 1)
                if h.has(-1):
                    other = 1 - par
                    rows = slice(other * HEAD_DIM, (other + 1) * HEAD_DIM)
                    shift = -1 - other
                    slot = h.pair_parity(shift)
                    pe.wait_ge(weight_masked, h(0))
                    if other == 0:
                        pe.wait_ge(v_rows_done, h.pair_count(shift, 1))
                        if not h.first(shift, 4):
                            pe.wait_ge(o_done, h.pair_count(shift, -1))
                    out, w = bank[2 + slot], weight[other]
                    v = v_rows[slot][:].rearrange("p (c d) -> p c d", c=3)
                    old = pv_now[slot]
                    nc.tensor.matmul(out[rows, 0:SEQ], v[:, 0, rows], w[:, S0:S0 + SEQ], start=True, stop=False)
                    nc.tensor.matmul(out[rows, P:SEQ], v[:, 1, rows], w[:, S1:S1 + P], start=False, stop=True)
                    nc.tensor.matmul(out[rows, SEQ:TOK], old[:, 0, rows], w[:, C0:C1], start=True, stop=False)
                    nc.tensor.matmul(out[rows, SEQ:TOK], old[:, 1, rows], w[:, C1:NW], start=False, stop=False)
                    nc.tensor.matmul(out[rows, SEQ:TOK], v[:, 2, rows], w[:, NW:S1], start=False, stop=True) \
                        .then_inc(mixed, 1)

            for phase in PHASES:
                stage, kind = phase.stage, phase.kind

                def step(turn, n, b, phase=phase, stage=stage, kind=kind):
                    i = index(turn, n, phase.body)
                    slot = b % 2
                    if kind == "qkv" and turn is None and n >= phase.groups - 2:
                        attn_step(Head(None, n - phase.groups), n % 2)
                    parts = index(turn, 2 * (n + phase.first_group), 2 * phase.body)
                    xg = xg_of(stage)
                    if kind in ("up", "qkv", "ple", "lru_u", "lru_g"):
                        if turn is not None or n >= 2:
                            pe.wait_ge(pair_free, index(turn, n + phase.first_pair - 1, phase.body))
                        else:
                            wait(pe, pair_free, phase.first_pair - 1 + n)
                            if phase.name == "up1":
                                pe.wait_ge(x_new, 8 * (stage - 1) + 6 + 2 * n)
                            if phase.name == "up3":
                                pe.wait_ge(x_new, 8 * (stage - 1) + 7 + n)
                    elif kind == "down" and b % 2 == 0:
                        wait(pe, x_new, index(turn, n // 2 + KD * stage - 1, phase.body // 2))
                    elif kind == "wo":
                        if n == 1:
                            pe.wait_ge(o_done, PAIRS)
                        wait(pe, x_new, 8 * stage + 2 * (n - 1) if n >= 2 else 0)
                    elif kind == "lru_o":
                        if turn is None and n < 2:
                            pe.wait_ge(pair_free, next(p for p in PHASES if p.name == "lru_g").first_pair + KR - 1 + n)
                        else:
                            pe.wait_ge(x_new, index(turn, n + KD * stage - 1, phase.body))

                    pair = [bank[2 * slot][:, 0:TOK], bank[2 * slot + 1][:, 0:TOK]]
                    if kind in ("up", "qkv"):
                        outs = [(pair[o], xg, range(KD), True, True) for o in range(2)]
                    elif kind == "wo":
                        outs = [(pair[o], (o_hi, o_lo), range(KD), True, True) for o in range(2)]
                    elif kind == "down":
                        half = b % 2
                        ks = range(half * KF // 2, (half + 1) * KF // 2)
                        outs = [(bank[4 + b // 2][:, 0:TOK], (h_hi, h_lo), ks, half == 0, half == 1)]
                    elif kind == "ple":
                        layer = int(phase.name[-1])
                        outs = [(pair[1], (p_hi, p_lo), range(layer * KP, (layer + 1) * KP), True, True),
                                (pair[0], xg, range(KD), True, True)]
                    elif kind in ("lru_u", "lru_g"):
                        outs = [(pair[0], xg, range(KD), True, True)]
                    elif kind == "lru_o":
                        outs = [(pair[0], (y_hi, y_lo), range(KR), True, True)]
                    else:
                        outs = [(bank[4 + (n * HALF + m) % 4][:, 0:CW], (c_hi, c_lo),
                                 [n // 2 * HALF + k for k in BAND[m]], True, True) for m in range(HALF)]

                    tile = 0
                    pe.wait_ge(w_lo_done, parts + 1)
                    for o, (out, operand, ks, opens, closes) in enumerate(outs):
                        if kind == "gates" and n * HALF + o >= 4:
                            pe.wait_ge(gate_read, n * HALF + o - 3)
                        for k in ks:
                            if tile == phase.part_a:
                                pe.wait_ge(w_lo_done, parts + 2)
                            if operand is xg and n == 0 and turn is None:
                                pe.wait_ge(xg_done, 8 * stage + k + 1)
                            if kind == "down" and turn is None and n < 2:
                                pe.wait_ge(hidden_lo_done, KF * int(phase.name[-1]) + k + 1)
                            if kind == "ple" and n == 0 and turn is None and operand[0] is p_hi:
                                pe.wait_ge(p_done, 1)
                            if kind == "wo" and n == 0 and o == 0:
                                pe.wait_ge(o_done, k + 1)
                            if kind == "gates":
                                pe.wait_ge(c_done, k + 1)
                            if kind == "lru_o" and n == 0 and turn is None:
                                pe.wait_ge(y_done, k + 1)
                            if kind in ("ple", "lru_u") and n == 0 and turn is None and tile == phase.tiles - 2:
                                mean(stage)
                            last = product(out, slot, tile, operand, k, CW if kind == "gates" else TOK,
                                           opens and k == ks[0], closes and k == ks[-1])
                            tile += 1
                        if kind == "gates" and o < HALF - 1:
                            last.then_inc(gate_summed, 1)
                        if n == 0 and turn is None and o == 0 and kind in ("up", "qkv"):
                            mean(stage)
                    last.then_inc(tiles_done, 1)

                run_groups(pe, phase, step)
                if phase.name == "qkv":
                    pe.wait_ge(attn_consts, 11)
                    run_heads(pe, attn_step)
            mean(STAGES - 1)


def next_group(phase, after, turn, n, b):
    if turn is not None or n + 2 < phase.groups:
        return phase, turn, n + 2, b + 2
    return None if after is None else (after, None, n + 2 - phase.groups, n + 2 - phase.groups)


def up_base(phase):
    return KF * int(phase.name[-1])


def gate_base(phase):
    base = 0
    for p in PHASES:
        if p is phase:
            return base
        base += p.groups if p.kind in ("up", "ple") else 0


class Head:

    def __init__(self, turn, n):
        self.turn, self.n = turn, n

    def __call__(self, k):
        if self.turn is None:
            return self.n + k
        return self.turn * 4 + (self.n + k)

    def has(self, k):
        return self.turn is not None or 0 <= self.n + k < HEADS

    def first(self, k, count=2):
        return self.turn is None and self.n + k < count

    def pair(self, k):
        if self.turn is None:
            return (self.n + k) // 2
        return self.turn * 2 + (self.n + k) // 2

    def pair_count(self, k, more):
        if self.turn is None:
            return (self.n + k) // 2 + more
        return self.turn * 2 + ((self.n + k) // 2 + more)

    def pair_parity(self, k):
        return (self.n + k) // 2 % 2


def run_heads(eng, step):
    first, tail = 5, 4
    for n in range(first):
        step(Head(None, n), n % 2)
    with eng.Fori(0, (HEADS + 1 - first - tail) // 4) as turn:
        for b in range(4):
            step(Head(turn, first + b), (first + b) % 2)
    for n in range(HEADS + 1 - tail, HEADS + 1):
        step(Head(None, n), n % 2)


def tiles(w):
    return w.reshape(w.shape[0] // P, P, w.shape[1] // P, P)


def by_output(w):
    return tiles(w).transpose(2, 1, 0, 3)


def chunks(v):
    v = v.reshape(*v.shape[:-1], v.shape[-1] // P, P)
    return np.moveaxis(v, -1, 0)


def by_token(prompt, sample):
    both = np.concatenate([prompt, sample], axis=0)
    return both.reshape(both.shape[0], -1, P).transpose(2, 1, 0)


def band_tiles(blocks):
    out = []
    side = HALF * P
    for half in range(2):
        full = np.zeros((side, side), blocks.dtype)
        for n in range(LRU_BLOCKS // 2):
            at = slice(n * LRU_BLOCK, (n + 1) * LRU_BLOCK)
            full[at, at] = blocks[half * LRU_BLOCKS // 2 + n]
        cut = tiles(full)
        out.append(np.concatenate([cut[k, :, m, :] for m in range(HALF) for k in BAND[m]], axis=1))
    return out


def flat(w):
    return w.reshape(w.shape[0], P, -1)


def layout(inputs):
    get = {k: np.asarray(v) for k, v in inputs.items()}
    up, down, ple = [], [], []
    for layer in range(2):
        for n in range(2):
            g, u = by_output(get["ffn_w_gate"][layer, n]), by_output(get["ffn_w_up"][layer, n])
            up.append(flat(np.stack([g, u], axis=2)))
            d = by_output(get["ffn_w_down"][layer, n])
            d = d.reshape(KD, P, 2, KF // 2, P).transpose(0, 2, 1, 3, 4)
            down.append(flat(d.reshape(2 * KD, P, KF // 2, P)))
        gate, proj = by_output(get["ple_w_gate"][layer]), by_output(get["ple_w_proj"][layer])
        ple.append(flat(np.concatenate([proj, gate], axis=2)))

    def two_outputs(w):
        w = by_output(w)
        return flat(w.reshape(w.shape[0] // 2, 2, P, *w.shape[2:]).transpose(0, 2, 1, 3, 4))

    w_in = get["lru_w_in"][0]
    band_a, band_x = band_tiles(get["lru_w_a"][0]), band_tiles(get["lru_w_x"][0])
    vecs = {
        "g": np.concatenate([get["norm_g"].reshape(8, D_MODEL), get["final_norm_g"][None]]),
        "conv_w": get["lru_conv_w"][0], "conv_b": get["lru_conv_b"][0], "b_a": get["lru_b_a"][0],
        "b_x": get["lru_b_x"][0], "lam": get["lru_lambda"][0], "h0": get["state_lru_h"][0, 0],
    }
    p = [by_token(get["p_prompt"][i, 0], get["p_sample"][i, 0]) for i in range(2)]
    past_k = get["cache_sb_k"][0, 0].reshape(PAST, PAIRS, P).transpose(2, 1, 0)
    past_v = get["cache_sb_v"][0, 0].reshape(PAST // P, P, D_MODEL).transpose(1, 0, 2)
    arrays = {
        "x": by_token(get["x_prompt"][0], get["x_sample"][0]),
        "p": np.concatenate(p, axis=1),
        "vecs": np.concatenate([chunks(vecs[n]).reshape(P, -1) for n in VECS], axis=1),
        "past_k": past_k, "past_v": past_v,
        "conv_state": chunks(get["state_lru_conv"][0, 0]).transpose(0, 2, 1),
        "up": np.concatenate(up), "down": np.concatenate(down), "ple": np.concatenate(ple),
        "qkv": two_outputs(get["sb_w_qkv"][0]), "wo": two_outputs(get["sb_w_o"][0]),
        "lru_u": flat(by_output(w_in[:, D_RNN:])), "lru_g": flat(by_output(w_in[:, :D_RNN])),
        "gates": np.stack([band_a[0], band_x[0], band_a[1], band_x[1]]),
        "lru_o": flat(by_output(get["lru_w_o"][0])),
    }
    return {k: np.ascontiguousarray(v) for k, v in arrays.items()}


_OUTS = {"y": (P, KD, TOK), "kv_new": (P, 2 * KD, TOK), "tails": (P, KR, 2 * HALO + 2)}


def kernel(**inputs):
    import concourse.bacc as _bacc
    from concourse.bass_utils import run_bass_kernel_spmd as _run

    nc = _bacc.Bacc("TRN2", target_bir_lowering=False, num_devices=1)
    arrays, aps = {}, {}
    for name, array in layout(inputs).items():
        arrays[f"in_{name}"] = array
        aps[name] = nc.dram_tensor(f"in_{name}", array.shape, mybir.dt.from_np(array.dtype), kind="ExternalInput").ap()
    for name, shape in _OUTS.items():
        aps[name] = nc.dram_tensor(f"out_{name}", shape, F32, kind="ExternalOutput").ap()
    build(nc, aps)
    r = _run(nc, [arrays], core_ids=[0]).results[0]

    y = np.asarray(r["out_y"]).transpose(2, 1, 0).reshape(TOK, D_MODEL)
    kv = np.asarray(r["out_kv_new"]).reshape(P, 2, KD, TOK).transpose(1, 3, 2, 0).reshape(2, TOK, HEADS, HEAD_DIM)
    tails = np.asarray(r["out_tails"]).transpose(2, 1, 0).reshape(2 * HALO + 2, D_RNN)
    return (y[None, :SEQ], y[None, SEQ:],
            kv[0][None, None, :SEQ], kv[1][None, None, :SEQ],
            tails[2 * HALO][None, None], tails[None, None, 0:HALO],
            kv[0][None, None, SEQ:], kv[1][None, None, SEQ:],
            tails[2 * HALO + 1][None, None], tails[None, None, HALO:2 * HALO])
```

```python
from contextlib import ExitStack

import concourse.bass as bass
import numpy as np
from concourse import mybir

F32 = mybir.dt.float32
F32R = mybir.dt.float32r
ALU = mybir.AluOpType
ACT = mybir.ActivationFunctionType

P = 128
D_MODEL = 1024
D_FF = 2816
D_RNN = 1280
PLE_DIM = 256
HEADS = 16
HEAD_DIM = D_MODEL // HEADS
SEQ = 256
DEC = 32
PAST = 256
CONV_W = 4
LRU_BLOCKS = 16
LRU_C = 8.0
EPS = 1e-6

TOK = SEQ + DEC
KD = D_MODEL // P
KF = D_FF // P
KR = D_RNN // P
KP = PLE_DIM // P
PAIRS = HEADS // 2
HALO = CONV_W - 1
EXT = HALO + SEQ + HALO + DEC + 1
CW = EXT - HALO
SAMPLE = SEQ + HALO
HALF = KR // 2
LRU_BLOCK = D_RNN // LRU_BLOCKS
BAND = [[k for k in range(HALF)
         if any(b * LRU_BLOCK < (k + 1) * P and (b + 1) * LRU_BLOCK > k * P
                and b * LRU_BLOCK < (m + 1) * P and (b + 1) * LRU_BLOCK > m * P for b in range(LRU_BLOCKS // 2))]
        for m in range(HALF)]
STAGES = 9
SQUARES_BEFORE = [0] + [KD // 2 - 1 + n * (KD - 1) for n in range(STAGES - 1)]
BAND_TILES = sum(map(len, BAND))
IN_FIRST = [(("u", 0), ("u", 1)), (("u", 2), ("u", 3)), (("u", 4), ("g", 0)),
            (("u", 5), ("u", 6)), (("u", 7), ("u", 8)), (("u", 9), ("g", 1))]
IN_LAST = [(("g", m), ("g", m + 1)) for m in range(2, KR, 2)]
U_OF = [[m for side, m in group if side == "u"] for group in IN_FIRST]
GELU_AT = [range(0, 6), range(6, 8), range(8, KR)]

C0, C1, NW, S1, S0, SCOLS = 0, DEC, 2 * DEC, 3 * DEC, 3 * DEC + P, 3 * DEC + P + SEQ
MASKED = slice(NW, S0 + P)

VECS = {"g": STAGES * KD, "conv_w": CONV_W * KR, "conv_b": KR, "b_a": KR, "b_x": KR, "lam": KR, "h0": KR}


class Phase:

    def __init__(self, name, stage, groups, tiles, body=2, head=0, counted=False):
        self.name, self.kind, self.stage, self.groups, self.tiles = name, name.rstrip("0123"), stage, groups, tiles
        self.body, self.head = body, head
        self.counted = counted
        self.part_a = (tiles + 1) // 2


def plan():
    def ffn(n, stage):
        return [Phase(f"up{n}", stage, KF, 2 * KD, head=2, counted=True),
                Phase(f"down{n}", stage, 2 * KD, KF // 2, body=4, head=4)]

    def ple(n, stage):
        return [Phase(f"ple{n}", stage, KD, KD + KP, head=2, counted=True)]

    phases = ffn(0, 0)
    phases += [Phase("qkv", 1, 3 * KD // 2, 2 * KD, head=2, counted=True), Phase("wo", 1, KD // 2, 2 * KD, body=4)]
    phases += ffn(1, 2) + ple(0, 3) + ffn(2, 4)
    phases += [Phase("lru_in", 5, len(IN_FIRST), 2 * KD, body=len(IN_FIRST), counted=True),
               Phase("gates", 5, 4, BAND_TILES, body=4),
               Phase("lru_g", 5, len(IN_LAST), 2 * KD, body=len(IN_LAST), counted=True),
               Phase("lru_o", 5, KD, KR, body=KD)]
    phases += ffn(3, 6) + ple(1, 7)
    group = pair = 0
    for p in phases:
        p.first_group, p.first_pair = group, pair
        group += p.groups
        pair += p.groups if p.counted else 0
    return phases


PHASES = plan()
WO = next(p for p in PHASES if p.name == "wo")
WO_SPLIT_AT = (13, 14)
FIRST_PIECES = [(range(0, KD // 4), (0, KD // 2)), (range(KD // 4, KD // 2), (KD // 2, KD)),
                (range(KD // 2, KD), (KD, 2 * KD))]


def run_groups(eng, phase, step):
    for n in range(phase.head):
        step(None, n, n % phase.body)
    turns = (phase.groups - phase.head) // phase.body - 1
    if turns > 0:
        with eng.Fori(0, turns) as turn:
            for b in range(phase.body):
                step(turn, phase.head + b, b)
    for n in range(phase.groups - phase.body, phase.groups):
        step(None, n, n % phase.body)


def index(turn, n, per_turn):
    return n if turn is None else turn * per_turn + n


def one(i):
    return slice(i, i + 1) if isinstance(i, int) else bass.ts(i, 1)


def wait(eng, sem, value):
    if not isinstance(value, int) or value > 0:
        eng.wait_ge(sem, value)


def build(nc, a):
    ctx = ExitStack()
    with ctx:
        def sb(name, shape, dt=F32, scope=ctx):
            return scope.enter_context(nc.sbuf_tensor(name, shape, dt))

        def sem(name):
            return ctx.enter_context(nc.semaphore(name))

        bank = [ctx.enter_context(nc.psum_tensor(f"bank{i}", [P, 512], F32)) for i in range(8)]

        x = sb("x_res", [P, KD, TOK])
        xg_main = (sb("xg_hi", [P, KD, TOK], F32R), sb("xg_lo", [P, KD, TOK], F32R))
        raw = [sb(f"raw{i}", [P, 2 * KD * P]) for i in range(2)]
        w_hi = [sb(f"w_hi{i}", [P, 2 * KD * P], F32R) for i in range(2)]
        w_lo = [sb(f"w_lo{i}", [P, 2 * KD * P], F32R) for i in range(2)]
        vecs = sb("vecs_sb", [P, sum(VECS.values())])
        vec, at = {}, 0
        for n, w in VECS.items():
            vec[n] = vecs[:, at:at + w]
            at += w
        gain = vec["g"].rearrange("p (s k) -> p s k", s=STAGES)
        p_hi = sb("p_hi", [P, 2 * KP, TOK], F32R)
        p_lo = sb("p_lo", [P, 2 * KP, TOK], F32R)
        square = sb("square", [P, TOK])
        last_square = sb("last_square", [P, TOK])
        sum_squares = sb("sum_squares", [P, TOK])
        std = sb("std", [P, TOK])
        rstd = sb("rstd", [P, TOK])
        gate_in = sb("gate_in", [P, TOK])
        gate_act = sb("gate_act", [P, TOK])
        up_in = sb("up_in", [P, TOK])
        hidden = [sb(f"hidden{i}", [P, TOK]) for i in range(2)]
        y_now = (*hidden, gate_in, gate_act, up_in)
        mean_w = sb("mean_w", [P, P])
        eps_col = sb("eps_col", [P, 1])
        series = sb("series", [P, 7, KR])
        decay = sb("decay", [P, KR])

        with ExitStack() as scope:
            h_hi = sb("h_hi", [P, KF, TOK], F32R, scope)
            h_lo = sb("h_lo", [P, KF, TOK], F32R, scope)
            xg_side = (sb("xg_side_hi", [P, KD, TOK], F32R, scope), sb("xg_side_lo", [P, KD, TOK], F32R, scope))
            p_raw = sb("p_raw", [P, 2 * KP, TOK], F32, scope)
            first_squares = sb("first_squares", [P, KD // 2, TOK], F32, scope)
        with ExitStack() as scope:
            o_hi = sb("o_hi", [P, KD, TOK], F32R, scope)
            o_lo = sb("o_lo", [P, KD, TOK], F32R, scope)
            qkv = sb("qkv_sb", [P, 3 * KD, TOK], F32, scope)
            past_k = sb("past_k_sb", [P, PAIRS, PAST], F32, scope)
            past_v = sb("past_v_sb", [P, PAST // P, D_MODEL], F32, scope)
            k_now = [sb(f"k_now{i}", [P, TOK + PAST], F32, scope) for i in range(2)]
            q_now = [sb(f"q_now{i}", [P, TOK], F32, scope) for i in range(2)]
            v_now = [sb(f"v_now{i}", [P, 3 * P], F32, scope) for i in range(2)]
            pv_now = [sb(f"pv_now{i}", [P, PAST // P, P], F32, scope) for i in range(2)]
            v_rows = [sb(f"v_rows{i}", [P, 3 * P], F32, scope) for i in range(2)]
            log_part = [sb(f"log_part{i}", [P, SCOLS], F32, scope) for i in range(2)]
            stay = [sb(f"stay{i}", [P, SCOLS], F32, scope) for i in range(2)]
            log_sig = [sb(f"log_sig{i}", [P, SCOLS], F32, scope) for i in range(2)]
            weight = [sb(f"weight{i}", [P, SCOLS], F32, scope) for i in range(2)]
            mask = sb("mask", [P, SCOLS], F32, scope)
            later = sb("later", [P, P], F32, scope)
            ones = sb("ones", [P, P], F32, scope)
            ident = sb("ident", [P, P], F32, scope)
        with ExitStack() as scope:
            y_hi = sb("y_hi", [P, KR, TOK], F32R, scope)
            with ExitStack() as inner:
                gate_g = sb("gate_g", [P, KR, TOK], F32, inner)
            y_lo = sb("y_lo", [P, KR, TOK], F32R, scope)
            c_hi = sb("c_hi", [P, KR, CW], F32R, scope)
            c_lo = sb("c_lo", [P, KR, CW], F32R, scope)
            u_ext = sb("u_ext", [P, KR, EXT], F32, scope)
            conv = sb("conv", [P, KR, CW], F32, scope)
            rate = sb("rate", [P, KR, CW], F32, scope)
            gated = sb("gated", [P, HALF, CW], F32, scope)
            a_square = sb("a_square", [P, HALF, CW], F32, scope)
            tails = sb("tails", [P, KR, 2 * HALO + 2], F32, scope)
        with ExitStack() as scope:
            y_rows = sb("y_rows", [P, KD, TOK], F32, scope)

        def xg_of(stage):
            return xg_side if stage == 4 else xg_main

        raw_landed = [sem("raw_landed0"), sem("raw_landed1")]
        raw_first = [sem("raw_first0"), sem("raw_first1")]
        first_hi_done, first_lo_done = sem("first_hi_done"), sem("first_lo_done")
        x_landed = [sem(f"x_landed{piece}") for piece in range(3)]
        vecs_landed, p_landed = sem("vecs_landed"), sem("p_landed")
        past_landed, state_landed = sem("past_landed"), sem("state_landed")
        kv_stored, tails_stored = sem("kv_stored"), sem("tails_stored")
        y_stored = sem("y_stored")
        w_hi_done, w_lo_done = sem("w_hi_done"), sem("w_lo_done")
        tiles_done = sem("tiles_done")
        pair_free = sem("pair_free")
        x_new, xg_hi_done, xg_done = sem("x_new"), sem("xg_hi_done"), sem("xg_done")
        squared, summed_squares, first_squared = sem("squared"), sem("summed_squares"), sem("first_squared")
        last_squared = sem("last_squared")
        consts, mean_done, std_done, rstd_done = sem("consts"), sem("mean_done"), sem("std_done"), sem("rstd_done")
        gate_in_done, gate_act_done = sem("gate_in_done"), sem("gate_act_done")
        hidden_done, hidden_hi_done, hidden_lo_done = sem("hidden_done"), sem("hidden_hi_done"), sem("hidden_lo_done")
        p_hi_done, p_done = sem("p_hi_done"), sem("p_done")
        decay_act, decay_dve = sem("decay_act"), sem("decay_dve")
        attn_consts = sem("attn_consts")
        kq_now_done, v_now_done = sem("kq_now_done"), sem("v_now_done")
        v_turned, v_rows_done = sem("v_turned"), sem("v_rows_done")
        scored, abs_done, exp_done, log_done = sem("scored"), sem("abs_done"), sem("exp_done"), sem("log_done")
        stay_done, log_sig_done, stay_masked = sem("stay_done"), sem("log_sig_done"), sem("stay_masked")
        later_summed, exponent_done = sem("later_summed"), sem("exponent_done")
        weight_done, weight_masked, mixed = sem("weight_done"), sem("weight_masked"), sem("mixed")
        o_hi_done, o_done = sem("o_hi_done"), sem("o_done")
        history_zero = sem("history_zero")
        conv_first, conv_step, c_hi_done, c_done = sem("conv_first"), sem("conv_step"), sem("c_hi_done"), sem("c_done")
        conv_tail = sem("conv_tail")
        gate_summed, gate_read = sem("gate_summed"), sem("gate_read")
        s_done, gated_used, tanh_done, a_done = sem("s_done"), sem("gated_used"), sem("tanh_done"), sem("a_done")
        a_square_done, b_square_done, b_root_done = sem("a_square_done"), sem("b_square_done"), sem("b_root_done")
        addend_done, late_addend_done = sem("addend_done"), sem("late_addend_done")
        h_done, gelu_done = sem("h_done"), sem("gelu_done")
        y_prod, y_hi_done, y_done = sem("y_prod"), sem("y_hi_done"), sem("y_done")
        tails_done = sem("tails_done")
        out_ready = sem("out_ready")

        def group_dram(phase, i):
            kind, layer_ffn = phase.kind, phase.name[-1]
            if kind in ("up", "down"):
                return a[kind][one(int(layer_ffn) * phase.groups + i)] if isinstance(i, int) else \
                    a[kind][one(i + int(layer_ffn) * phase.groups)]
            if kind == "ple":
                return a[kind][one(i + int(layer_ffn) * phase.groups)]
            return a[phase.name][one(i)]

        block = ctx.enter_context(nc.Block())

        @block.sync
        def _(sp):
            sp.dma_start(vecs[:], a["vecs"]).then_inc(vecs_landed, 16)
            first = PHASES[0]
            for piece, (ks, (lo, hi)) in enumerate(FIRST_PIECES):
                sp.dma_start(x[:, ks[0]:ks[-1] + 1, :], a["x"][:, ks[0]:ks[-1] + 1, :]).then_inc(x_landed[piece], 16)
                sp.dma_start(raw[0][:, lo * P:hi * P], group_dram(first, 0)[0, :, lo * P:hi * P]) \
                    .then_inc((*raw_first, raw_landed[0])[piece], 16)

            for phase in PHASES:
                def load(turn, n, b, phase=phase):
                    i = index(turn, n, phase.body)
                    if n == 0 and turn is None and phase is first:
                        return
                    wait(sp, w_lo_done, index(turn, 2 * (n + phase.first_group - 1), 2 * phase.body))
                    sp.dma_start(raw[b % 2][:, 0:phase.tiles * P],
                                 group_dram(phase, i).rearrange("a p c -> (a p) c")).then_inc(raw_landed[b % 2], 16)

                    if n == 1 and turn is None and phase is first:
                        sp.dma_start(p_raw[:], a["p"]).then_inc(p_landed, 16)

                run_groups(sp, phase, load)

            for k in range(KD):
                sp.wait_ge(out_ready, k + 1)
                sp.dma_start(a["y"][:, k, :], y_rows[:, k, :]).then_inc(y_stored, 16)
            sp.wait_ge(y_stored, 16 * KD)

        @block.gpsimd
        def _(pool):
            nc.gpsimd.memset(mean_w[:], 1.0 / D_MODEL).then_inc(consts, 1)
            nc.gpsimd.memset(eps_col[:], EPS).then_inc(consts, 1)

            def add_square(k, stage, term):
                nc.gpsimd.tensor_tensor(sum_squares[:], sum_squares[:], term, ALU.add).then_inc(summed_squares, 1)

            def square_of(k, stage):
                nc.gpsimd.tensor_tensor(square[:], x[:, k, :], x[:, k, :], ALU.mult).then_inc(squared, 1)
                pool.wait_ge(squared, k + SQUARES_BEFORE[stage])

            def squares(stage):
                pool.wait_ge(mean_done, stage)
                pool.wait_ge(x_new, (stage - 1) * KD + 1)
                nc.gpsimd.tensor_tensor(sum_squares[:], x[:, 0, :], x[:, 0, :], ALU.mult).then_inc(summed_squares, 1)
                with pool.Fori(1, KD - (stage == STAGES - 1)) as k:
                    pool.wait_ge(x_new, k + ((stage - 1) * KD + 1))
                    pool.wait_ge(summed_squares, k + stage * KD)
                    square_of(k, stage)
                    add_square(k, stage, square[:])

            for landed in x_landed[0:2]:
                pool.wait_ge(landed, 16)
            nc.gpsimd.tensor_tensor(sum_squares[:], x[:, 0, :], x[:, 0, :], ALU.mult).then_inc(summed_squares, 1)
            for k in range(1, KD):
                pool.wait_ge(summed_squares, k)
                if k < KD // 2:
                    square_of(k, 0)
                elif k == KD // 2:
                    pool.wait_ge(first_squared, 1)
                add_square(k, 0, square[:] if k < KD // 2 else first_squares[:, k - KD // 2, :])
            squares(1)

            pool.wait_ge(x_new, KD)
            pool.dma_start(past_k[:], a["past_k"]).then_inc(past_landed, 16)
            pool.dma_start(past_v[:], a["past_v"]).then_inc(past_landed, 16)
            nc.gpsimd.memset(ones[:], 1.0).then_inc(attn_consts, 1)
            nc.gpsimd.memset(later[:], 1.0).then_inc(attn_consts, 1)
            nc.gpsimd.memset(ident[:], 0.0).then_inc(attn_consts, 1)
            nc.gpsimd.memset(mask[:], 1.0).then_inc(attn_consts, 1)
            for i in range(2):
                nc.gpsimd.memset(v_now[i][:], 0.0).then_inc(attn_consts, 1)
            pool.wait_ge(attn_consts, 6)
            nc.gpsimd.affine_select(out=later[:], in_=later[:], compare_op=ALU.is_gt, fill=0.0, base=0,
                                    pattern=[[-1, P]], channel_multiplier=1).then_inc(attn_consts, 1)
            nc.gpsimd.affine_select(out=ident[:], in_=ident[:], compare_op=ALU.not_equal, fill=1.0, base=0,
                                    pattern=[[-1, P]], channel_multiplier=1).then_inc(attn_consts, 1)
            for lo, n in ((S0, P), (S1, P), (NW, DEC)):
                nc.gpsimd.affine_select(out=mask[:, lo:lo + n], in_=mask[:, lo:lo + n], compare_op=ALU.is_gt,
                                        fill=0.0, base=0, pattern=[[1, n]], channel_multiplier=-1) \
                    .then_inc(attn_consts, 1)

            pool.wait_ge(attn_consts, 11)

            def attn_step(h, par):
                if h.has(2):
                    pool.wait_ge(stay_done, h(3))
                    nc.gpsimd.tensor_tensor(stay[par][:, MASKED], stay[par][:, MASKED], mask[:, MASKED], ALU.mult).then_inc(stay_masked, 1)
                if h.has(0):
                    pool.wait_ge(weight_done, h(1))
                    nc.gpsimd.tensor_tensor(weight[par][:, MASKED], weight[par][:, MASKED], mask[:, MASKED], ALU.mult) \
                        .then_inc(weight_masked, 1)

            attn_step(Head(None, -2), 0)
            attn_step(Head(None, -1), 1)
            qkv_phase = next(p for p in PHASES if p.name == "qkv")
            pool.wait_ge(pair_free, qkv_phase.first_pair + qkv_phase.groups)
            pool.dma_start(a["kv_new"], qkv[:, KD:3 * KD, :]).then_inc(kv_stored, 16)
            run_heads(pool, attn_step)

            for stage in range(2, 6):
                squares(stage)

            pool.wait_ge(x_new, 5 * KD)
            nc.gpsimd.memset(u_ext[:, :, 0:HALO], 0.0).then_inc(history_zero, 1)
            nc.gpsimd.memset(u_ext[:, :, EXT - 1:EXT], 0.0).then_inc(history_zero, 1)
            pool.dma_start(u_ext[:, :, SAMPLE:SAMPLE + HALO], a["conv_state"]).then_inc(state_landed, 16)

            with pool.Fori(0, KR) as m:
                pool.wait_ge(c_hi_done, m + 1)
                nc.gpsimd.tensor_tensor(c_lo[:, m, :], conv[:, m, :], c_hi[:, m, :].bitcast(F32), ALU.subtract) \
                    .then_inc(c_done, 1)

            for half in range(2):
                pool.wait_ge(a_done, half + 1)
                if half == 1:
                    pool.wait_ge(gated_used, 2)
                for m in range(HALF):
                    nc.gpsimd.tensor_tensor((a_square, gated)[half][:, m, :], rate[:, half * HALF + m, :],
                                            rate[:, half * HALF + m, :], ALU.mult).then_inc(a_square_done, 1)
            pool.wait_ge(b_root_done, 2)

            def late_addend(m):
                nc.gpsimd.tensor_tensor(conv[:, m, :], conv[:, m, :], u_ext[:, m, 0:CW], ALU.mult) \
                    .then_inc(late_addend_done, 1)

            for m in range(HALF, KR - 2):
                late_addend(m)
            for m in range(KR):
                if m == HALF:
                    for late in range(KR - 2, KR):
                        late_addend(late)
                pool.wait_ge(gelu_done, next(n + 1 for n, ms in enumerate(GELU_AT) if m in ms))
                pool.wait_ge(h_done, m + 1)
                if m >= HALF:
                    pool.wait_ge(y_done, m - HALF + 1)
                nc.gpsimd.tensor_tensor(y_now[m % HALF][:], u_ext[:, m, 0:TOK], gate_g[:, m, :], ALU.mult) \
                    .then_inc(y_prod, 1)

            pool.wait_ge(tails_done, 4)
            pool.dma_start(a["tails"], tails[:]).then_inc(tails_stored, 16)
            for stage in range(6, 9):
                squares(stage)
            pool.wait_ge(kv_stored, 16)
            pool.wait_ge(tails_stored, 16)

        @block.scalar
        def _(act):
            def w_split(target, part):
                phase, turn, n, b = target
                slot = b % 2
                loads = index(turn, phase.first_group // 2 + n // 2 + 1, phase.body // 2)
                cols = slice(0, phase.part_a * P) if part == 0 else slice(phase.part_a * P, phase.tiles * P)
                if part == 0:
                    act.wait_ge(raw_landed[slot], loads * 16)
                    wait(act, tiles_done, index(turn, n + phase.first_group - 1, phase.body))
                nc.scalar.activation(w_hi[slot][:, cols], raw[slot][:, cols], ACT.Copy).then_inc(w_hi_done, 1)

            def xg_high(stage, k, from_x_new=True):
                if from_x_new:
                    act.wait_ge(x_new, k + ((stage - 1) * KD + 1))
                nc.scalar.activation(xg_of(stage)[0][:, k, :], x[:, k, :], ACT.Copy, scale=gain[:, stage, one(k)]) \
                    .then_inc(xg_hi_done, 1)

            def root(stage):
                act.wait_ge(mean_done, stage + 1)
                nc.scalar.activation(std[:], bank[7][:, 0:TOK], ACT.Sqrt, bias=eps_col[:]).then_inc(std_done, 1)

            nc.scalar.preload_act_table_set("silu_and_others")
            act.wait_ge(vecs_landed, 16)
            for piece, (ks, (lo, hi)) in enumerate(FIRST_PIECES):
                act.wait_ge(x_landed[piece], 16)
                for k in ks:
                    xg_high(0, k, from_x_new=False)
                act.wait_ge((*raw_first, raw_landed[0])[piece], 16)
                nc.scalar.activation(w_hi[0][:, lo * P:hi * P], raw[0][:, lo * P:hi * P], ACT.Copy) \
                    .then_inc(w_hi_done if piece > 0 else first_hi_done, 1)
            nc.scalar.activation(first_squares[:], x[:, KD // 2:KD, :], ACT.Square).then_inc(first_squared, 1)
            for part in range(2):
                w_split((PHASES[0], None, 1, 1), part)
            act.wait_ge(consts, 2)

            def attn_step(h, par):
                if h.has(2):
                    act.wait_ge(scored, h(3))
                    if not h.first(2):
                        act.wait_ge(log_sig_done, h(1))
                    nc.scalar.activation(log_part[par][:], bank[4 + par][:, 0:SCOLS], ACT.Abs).then_inc(abs_done, 1)
                    act.wait_ge(abs_done, h(3))
                    nc.scalar.activation(log_part[par][:], log_part[par][:], ACT.Exp, scale=-1.0).then_inc(exp_done, 1)
                    act.wait_ge(exp_done, h(3))
                    nc.scalar.activation(log_part[par][:], log_part[par][:], ACT.Ln, bias=1.0).then_inc(log_done, 1)
                if h.has(0):
                    act.wait_ge(exponent_done, h(1))
                    nc.scalar.activation(weight[par][:], weight[par][:], ACT.Exp).then_inc(weight_done, 1)
                if par == 0 and h.has(-2):
                    c = h.pair(-2)
                    act.wait_ge(mixed, h(0))
                    nc.scalar.activation(o_hi[:, c, :], bank[2 + h.pair_parity(-2)][:, 0:TOK], ACT.Copy) \
                        .then_inc(o_hi_done, 1)
                if h.turn is None and h.n in WO_SPLIT_AT:
                    w_split((WO, None, 1, 1), WO_SPLIT_AT.index(h.n))

            for at_phase, phase in enumerate(PHASES):
                after = PHASES[at_phase + 1] if at_phase + 1 < len(PHASES) else None
                stage, kind = phase.stage, phase.kind

                def step(turn, n, b, phase=phase, after=after, stage=stage, kind=kind):
                    i = index(turn, n, phase.body)
                    nxt = next_group(phase, after, turn, n, b)
                    if kind == "qkv" and turn is None and n == phase.groups - 2:
                        nc.scalar.preload_act_table_set("natural_log_exp_and_others")
                        attn_step(Head(None, -2), 0)
                        attn_step(Head(None, -1), 1)
                    if n == 0 and turn is None and kind in ("up", "qkv", "ple", "lru_in"):
                        root(stage)
                    if n == 0 and turn is None and phase.name == "up1":
                        act.wait_ge(kv_stored, 16)
                    if n == 0 and turn is None and phase.name == "up3":
                        act.wait_ge(tails_stored, 16)
                    if kind == "up":
                        part(nxt, 0)
                        act.wait_ge(gate_in_done, gate_base(phase) + 1 + i)
                        nc.scalar.activation(gate_act[:], gate_in[:], ACT.Silu).then_inc(gate_act_done, 1)
                        part(nxt, 1)
                        act.wait_ge(hidden_done, up_base(phase) + 1 + i)
                        nc.scalar.activation(h_hi[:, i, :], hidden[b % 2][:], ACT.Copy).then_inc(hidden_hi_done, 1)
                        if phase.name == "up0" and turn is None and n == 1:
                            act.wait_ge(p_landed, 16)
                            nc.scalar.activation(p_hi[:], p_raw[:], ACT.Copy).then_inc(p_hi_done, 1)
                    elif kind == "down":
                        if b % 2 == 1:
                            xg_high(stage + 1, index(turn, n // 2, phase.body // 2))
                        part(nxt, 0)
                        part(nxt, 1)
                    elif kind == "qkv":
                        if turn is not None or n < phase.groups - 1:
                            part(nxt, 0)
                            part(nxt, 1)
                        if turn is None and n == 1:
                            nc.scalar.activation(series[:, 1, :], series[:, 0, :], ACT.Exp, scale=-1.0) \
                                .then_inc(decay_act, 1)
                    elif kind == "wo":
                        for o in range(2):
                            xg_high(stage + 1, 2 * n + o)
                        part(nxt, 0)
                        part(nxt, 1)
                    elif kind == "ple":
                        if stage + 1 < STAGES - 1 and (turn is not None or n > 0):
                            xg_high(stage + 1, index(turn, n - 1, phase.body))
                        if turn is not None or n < phase.groups - 1:
                            part(nxt, 0)
                        act.wait_ge(gate_in_done, gate_base(phase) + 1 + i)
                        nc.scalar.activation(gate_act[:], gate_in[:], ACT.Sigmoid).then_inc(gate_act_done, 1)
                        if turn is not None or n < phase.groups - 1:
                            part(nxt, 1)
                        if turn is None and n == phase.groups - 1:
                            if stage + 1 < STAGES - 1:
                                xg_high(stage + 1, n)
                            part(nxt, 0)
                            part(nxt, 1)
                    elif kind == "lru_in":
                        if n == phase.groups - 1:
                            nc.scalar.preload_act_table_set("sigmoid_and_others")
                        part(nxt, 0)
                        part(nxt, 1)
                        if n == 0:
                            act.wait_ge(history_zero, 2)
                            act.wait_ge(state_landed, 16)
                        act.wait_ge(pair_free, phase.first_pair + 1 + n)
                        for m in U_OF[n]:
                            nc.scalar.activation(conv[:, m, :], u_ext[:, m, 0:CW], ACT.Identity,
                                                 bias=vec["conv_b"][:, one(m)], scale=vec["conv_w"][:, one(m)]) \
                                .then_inc(conv_first, 1)
                        conv_high(n - 1)
                    elif kind == "gates":
                        half, is_x = n // 2, n % 2
                        ms = slice(half * HALF, (half + 1) * HALF)
                        if n == 3:
                            act.wait_ge(gated_used, 1)
                        for m in range(HALF):
                            q = n * HALF + m
                            if m < HALF - 1:
                                act.wait_ge(gate_summed, n * (HALF - 1) + m + 1)
                            else:
                                part(nxt, 0)
                                part(nxt, 1)
                                if n == 0:
                                    conv_high(len(IN_FIRST) - 1)
                                act.wait_ge(tiles_done, phase.first_group + n + 1)
                            chunk = half * HALF + m
                            dst = gated[:, m, :] if is_x else rate[:, chunk, :]
                            bias = vec["b_x" if is_x else "b_a"][:, chunk:chunk + 1]
                            nc.scalar.activation(dst, bank[(4 + q) % 8][:, 0:CW], ACT.Sigmoid, bias=bias) \
                                .then_inc(gate_read, 1)
                        if is_x:
                            tanh_s(half)
                        if n == 3:
                            decayed(0)
                    elif kind == "lru_g":
                        part(nxt, 0)
                        part(nxt, 1)
                        if n == 0:
                            decayed(1)
                        if n == 1:
                            b_root(0)
                            b_root(1)
                        if n >= 1:
                            gelu(phase, n)
                        if n >= 2:
                            for m in range((n - 2) * HALF, (n - 1) * HALF):
                                y_high(m)
                    elif kind == "lru_o":
                        for m in o_chunks(n):
                            xg_high(stage + 1, m)
                        part(nxt, 0)
                        part(nxt, 1)

                def part(nxt, which):
                    if nxt is not None:
                        w_split(nxt, which)

                def tanh_s(half):
                    ms = slice(half * HALF, (half + 1) * HALF)
                    act.wait_ge(conv_tail, 2)
                    act.wait_ge(s_done, half + 1)
                    nc.scalar.activation(u_ext[:, ms, 0:CW], rate[:, ms, :], ACT.Tanh).then_inc(tanh_done, 1)

                def decayed(half):
                    ms = slice(half * HALF, (half + 1) * HALF)
                    act.wait_ge(tanh_done, half + 1)
                    nc.scalar.activation(rate[:, ms, :], rate[:, ms, :], ACT.Exp, scale=-1.0).then_inc(a_done, 1)

                def b_root(half):
                    ms = slice(half * HALF, (half + 1) * HALF)
                    act.wait_ge(b_square_done, half + 1)
                    nc.scalar.activation(u_ext[:, ms, 0:CW], u_ext[:, ms, 0:CW], ACT.Sqrt).then_inc(b_root_done, 1)

                def gelu(phase, n):
                    ms = slice(GELU_AT[n - 1][0], GELU_AT[n - 1][-1] + 1)
                    act.wait_ge(pair_free, phase.first_pair + n + 1)
                    nc.scalar.activation(gate_g[:, ms, :], gate_g[:, ms, :], ACT.Gelu_apprx_tanh).then_inc(gelu_done, 1)

                def conv_high(n):
                    for j, m in enumerate(U_OF[n] if n >= 0 else ()):
                        act.wait_ge(conv_step, taps_before(n, HALO, j) + 1)
                        nc.scalar.activation(c_hi[:, m, :], conv[:, m, :], ACT.Copy).then_inc(c_hi_done, 1)

                def y_high(m):
                    act.wait_ge(y_prod, m + 1)
                    nc.scalar.activation(y_hi[:, m, :], y_now[m % HALF][:], ACT.Copy).then_inc(y_hi_done, 1)

                run_groups(act, phase, step)

                if phase.name == "up0":
                    nc.scalar.activation(series[:, 0, :], vec["lam"], ACT.Abs).then_inc(decay_act, 1)
                    act.wait_ge(decay_act, 1)
                if phase.name == "qkv":
                    run_heads(act, attn_step)
            act.wait_ge(x_new, (STAGES - 1) * KD)
            nc.scalar.activation(last_square[:], x[:, KD - 1, :], ACT.Square).then_inc(last_squared, 1)
            root(STAGES - 1)

        @block.vector
        def _(dve):
            def w_split(target, which):
                phase, turn, n, b = target
                slot = b % 2
                cols = slice(0, phase.part_a * P) if which == 0 else slice(phase.part_a * P, phase.tiles * P)
                dve.wait_ge(w_hi_done, index(turn, 2 * (n + phase.first_group) + 1 + which, 2 * phase.body))
                nc.vector.tensor_tensor(w_lo[slot][:, cols], raw[slot][:, cols], w_hi[slot][:, cols].bitcast(F32),
                                        ALU.subtract).then_inc(w_lo_done, 1)

            def part(nxt, which):
                if nxt is not None:
                    w_split(nxt, which)

            def low_part(dst, src, hi, scalar, done):
                nc.vector.scalar_tensor_tensor(out=dst, in0=src, scalar=scalar, in1=hi.bitcast(F32), op0=ALU.mult,
                                               op1=ALU.subtract).then_inc(done, 1)

            def xg_low(stage, k):
                hi, lo = xg_of(stage)
                dve.wait_ge(xg_hi_done, k + (stage * KD + 1))
                low_part(lo[:, k, :], x[:, k, :], hi[:, k, :], gain[:, stage, one(k)], xg_done)

            def inverse(stage):
                dve.wait_ge(std_done, stage + 1)
                nc.vector.reciprocal(rstd[:], std[:]).then_inc(rstd_done, 1)
                dve.wait_ge(rstd_done, stage + 1)

            def add_to_x(k, product, factor):
                nc.vector.scalar_tensor_tensor(out=x[:, k, :], in0=product, scalar=factor, in1=x[:, k, :],
                                               op0=ALU.mult, op1=ALU.add).then_inc(x_new, 1)

            dve.wait_ge(vecs_landed, 16)
            for piece, (ks, (lo, hi)) in enumerate(FIRST_PIECES):
                for k in ks:
                    xg_low(0, k)
                if piece == 0:
                    dve.wait_ge(first_hi_done, 1)
                else:
                    dve.wait_ge(w_hi_done, piece)
                nc.vector.tensor_tensor(w_lo[0][:, lo * P:hi * P], raw[0][:, lo * P:hi * P],
                                        w_hi[0][:, lo * P:hi * P].bitcast(F32), ALU.subtract) \
                    .then_inc(w_lo_done if piece > 0 else first_lo_done, 1)
            for which in range(2):
                w_split((PHASES[0], None, 1, 1), which)

            def stage_kq(pair, slot):
                nc.vector.tensor_scalar(q_now[slot][:], qkv[:, pair, :], HEAD_DIM ** -0.5, None, ALU.mult)
                nc.vector.tensor_copy(k_now[slot][:, 0:TOK], qkv[:, pair + KD, :])
                nc.vector.tensor_copy(k_now[slot][:, TOK:TOK + PAST], past_k[:, pair, :]).then_inc(kq_now_done, 1)

            def stage_v(pair, slot):
                nc.vector.tensor_copy(v_now[slot][:, 0:TOK], qkv[:, pair + 2 * KD, :])
                nc.vector.tensor_copy(pv_now[slot][:], past_v[:, :, bass.ts(pair, P)]).then_inc(v_now_done, 1)

            def attn_step(h, par):
                if par == 0 and h.has(0):
                    slot = h.pair_parity(0)
                    dve.wait_ge(v_turned, h.pair_count(0, 1))
                    nc.vector.tensor_copy(v_rows[slot][:], bank[0][:, 0:3 * P]).then_inc(v_rows_done, 1)
                if par == 1 and h.has(3):
                    stage_kq(h.pair(3), h.pair_parity(3))
                if h.has(0):
                    dve.wait_ge(later_summed, h(1))
                    if not h.first(0):
                        dve.wait_ge(mixed, h(-1))
                    nc.vector.tensor_tensor(weight[par][:], log_sig[par][:], bank[6 + par][:, 0:SCOLS], ALU.subtract) \
                        .then_inc(exponent_done, 1)
                if h.has(2):
                    dve.wait_ge(log_done, h(3))
                    if not h.first(2):
                        dve.wait_ge(later_summed, h(1))
                    scores = bank[4 + par][:, 0:SCOLS]
                    nc.vector.scalar_tensor_tensor(out=stay[par][:], in0=scores, scalar=0.0, in1=log_part[par][:],
                                                   op0=ALU.max, op1=ALU.add).then_inc(stay_done, 1)
                    if not h.first(2):
                        dve.wait_ge(exponent_done, h(1))
                    nc.vector.scalar_tensor_tensor(out=log_sig[par][:], in0=scores, scalar=0.0, in1=log_part[par][:],
                                                   op0=ALU.min, op1=ALU.subtract).then_inc(log_sig_done, 1)
                if par == 0 and h.has(-2):
                    c = h.pair(-2)
                    dve.wait_ge(o_hi_done, h.pair_count(-2, 1))
                    nc.vector.tensor_tensor(o_lo[:, c, :], bank[2 + h.pair_parity(-2)][:, 0:TOK],
                                            o_hi[:, c, :].bitcast(F32), ALU.subtract).then_inc(o_done, 1)
                if par == 1 and h.has(1):
                    stage_v(h.pair(1), h.pair_parity(1))
                if h.turn is None and h.n in WO_SPLIT_AT:
                    w_split((WO, None, 1, 1), WO_SPLIT_AT.index(h.n))

            def decay_rates():
                steps = [0]

                def link(ins):
                    steps[0] += 1
                    ins.then_inc(decay_dve, 1)
                    dve.wait_ge(decay_dve, steps[0])

                dve.wait_ge(decay_act, 2)
                e, t, z, z2, poly = (series[:, n, :] for n in (1, 2, 3, 4, 5))
                link(nc.vector.tensor_scalar(t, e, 2.0, None, ALU.add))
                link(nc.vector.reciprocal(t, t))
                link(nc.vector.tensor_tensor(z, e, t, ALU.mult))
                link(nc.vector.tensor_tensor(z2, z, z, ALU.mult))
                link(nc.vector.tensor_scalar(poly, z2, 1.0 / 17, 1.0 / 15, ALU.mult, ALU.add))
                for n in (13, 11, 9, 7, 5, 3, 1):
                    link(nc.vector.tensor_tensor(poly, poly, z2, ALU.mult))
                    link(nc.vector.tensor_scalar(poly, poly, 1.0 / n, None, ALU.add))
                link(nc.vector.tensor_tensor(poly, poly, z, ALU.mult))
                link(nc.vector.tensor_scalar(t, vec["lam"], -1.0, 0.0, ALU.mult, ALU.max))
                link(nc.vector.scalar_tensor_tensor(out=t, in0=poly, scalar=2.0, in1=t, op0=ALU.mult, op1=ALU.add))
                link(nc.vector.tensor_scalar(decay[:], t, LRU_C, None, ALU.mult))

            def taps(n, tap):
                for j, m in enumerate(U_OF[n] if n >= 0 else ()):
                    if tap == 1:
                        dve.wait_ge(conv_first, m + 1)
                    else:
                        dve.wait_ge(conv_step, taps_before(n, tap - 1, j) + 1)
                    nc.vector.scalar_tensor_tensor(out=conv[:, m, :], in0=u_ext[:, m, tap:tap + CW],
                                                   scalar=vec["conv_w"][:, one(tap * KR + m)], in1=conv[:, m, :],
                                                   op0=ALU.mult, op1=ALU.add).then_inc(conv_step, 1)

            def y_low(m):
                dve.wait_ge(y_hi_done, m + 1)
                nc.vector.tensor_tensor(y_lo[:, m, :], y_now[m % HALF][:], y_hi[:, m, :].bitcast(F32), ALU.subtract) \
                    .then_inc(y_done, 1)

            def scan(m):
                if m < HALF:
                    dve.wait_ge(addend_done, 1)
                else:
                    dve.wait_ge(late_addend_done, m - HALF + 1)
                nc.vector.tensor_tensor_scan(u_ext[:, m, 0:SEQ], rate[:, m, 0:SEQ], conv[:, m, 0:SEQ], 0.0,
                                             ALU.mult, ALU.add)
                nc.vector.tensor_tensor_scan(u_ext[:, m, SEQ:TOK], rate[:, m, SAMPLE:SAMPLE + DEC],
                                             conv[:, m, SAMPLE:SAMPLE + DEC], vec["h0"][:, m:m + 1],
                                             ALU.mult, ALU.add).then_inc(h_done, 1)

            def b_square(half):
                ms = slice(half * HALF, (half + 1) * HALF)
                dve.wait_ge(a_square_done, (half + 1) * HALF)
                nc.vector.scalar_tensor_tensor(out=u_ext[:, ms, 0:CW], in0=(a_square, gated)[half][:], scalar=1.0,
                                               in1=u_ext[:, ms, 0:CW], op0=ALU.add, op1=ALU.mult) \
                    .then_inc(b_square_done, 1)

            def addend():
                ms = slice(0, HALF)
                dve.wait_ge(b_root_done, 1)
                dve.wait_ge(gated_used, 1)
                nc.vector.tensor_tensor(conv[:, ms, :], conv[:, ms, :], u_ext[:, ms, 0:CW], ALU.mult) \
                    .then_inc(addend_done, 1)

            for at_phase, phase in enumerate(PHASES):
                after = PHASES[at_phase + 1] if at_phase + 1 < len(PHASES) else None
                stage, kind = phase.stage, phase.kind

                def step(turn, n, b, phase=phase, after=after, stage=stage, kind=kind):
                    i = index(turn, n, phase.body)
                    nxt = next_group(phase, after, turn, n, b)
                    if kind == "qkv" and turn is None and n == phase.groups - 2:
                        dve.wait_ge(pair_free, phase.first_pair + n)
                        dve.wait_ge(past_landed, 32)
                        dve.wait_ge(attn_consts, 11)
                        stage_kq(0, 0)
                    if n == 0 and turn is None and kind in ("up", "qkv", "ple", "lru_in"):
                        inverse(stage)
                    if n == 0 and turn is None and phase.name == "up1":
                        dve.wait_ge(kv_stored, 16)
                    if n == 0 and turn is None and phase.name == "up3":
                        dve.wait_ge(tails_stored, 16)
                    first, second = (bank[b % 2 * 2 + o][:, 0:TOK] for o in range(2))
                    if kind != "gates" and not (kind == "down" and b % 2 == 0) and not (kind == "lru_o" and n < 2):
                        dve.wait_ge(tiles_done, phase.first_group + 1 + i)
                    if kind == "up":
                        nc.vector.tensor_tensor(gate_in[:], first, rstd[:], ALU.mult).then_inc(gate_in_done, 1)
                        nc.vector.tensor_tensor(up_in[:], second, rstd[:], ALU.mult).then_inc(pair_free, 1)
                        part(nxt, 0)
                        dve.wait_ge(gate_act_done, gate_base(phase) + 1 + i)
                        dve.wait_ge(pair_free, phase.first_pair + 1 + i)
                        nc.vector.tensor_tensor(hidden[b % 2][:], gate_act[:], up_in[:], ALU.mult) \
                            .then_inc(hidden_done, 1)
                        part(nxt, 1)
                        dve.wait_ge(hidden_hi_done, up_base(phase) + 1 + i)
                        nc.vector.tensor_tensor(h_lo[:, i, :], hidden[b % 2][:], h_hi[:, i, :].bitcast(F32),
                                                ALU.subtract).then_inc(hidden_lo_done, 1)
                        if phase.name == "up0" and turn is None and n == 1:
                            dve.wait_ge(p_hi_done, 1)
                            nc.vector.tensor_tensor(p_lo[:], p_raw[:], p_hi[:].bitcast(F32), ALU.subtract) \
                                .then_inc(p_done, 1)
                    elif kind == "down":
                        if b % 2 == 1:
                            j = index(turn, n // 2, phase.body // 2)
                            add_to_x(j, bank[4 + b // 2][:, 0:TOK], 0.5)
                            xg_low(stage + 1, j)
                        part(nxt, 0)
                        part(nxt, 1)
                    elif kind == "qkv":
                        nc.vector.tensor_tensor(qkv[:, i * 2, :], first, rstd[:], ALU.mult)
                        nc.vector.tensor_tensor(qkv[:, i * 2 + 1, :], second, rstd[:], ALU.mult).then_inc(pair_free, 1)
                        if turn is None and n == phase.groups - 2:
                            attn_step(Head(None, -2), 0)
                            attn_step(Head(None, -1), 1)
                        if turn is not None or n < phase.groups - 1:
                            part(nxt, 0)
                            part(nxt, 1)
                        if turn is None and n == 1:
                            decay_rates()
                    elif kind == "wo":
                        for o, product in enumerate((first, second)):
                            add_to_x(2 * n + o, product, 1.0)
                        for o in range(2):
                            xg_low(stage + 1, 2 * n + o)
                        part(nxt, 0)
                        part(nxt, 1)
                    elif kind == "ple":
                        nc.vector.tensor_tensor(gate_in[:], first, rstd[:], ALU.mult).then_inc(gate_in_done, 1)
                        if stage + 1 < STAGES - 1 and (turn is not None or n > 0):
                            xg_low(stage + 1, index(turn, n - 1, phase.body))
                        if turn is not None or n < phase.groups - 1:
                            part(nxt, 0)
                        dve.wait_ge(gate_act_done, gate_base(phase) + 1 + i)
                        nc.vector.tensor_tensor(hidden[b % 2][:], gate_act[:], second, ALU.mult).then_inc(pair_free, 1)
                        dve.wait_ge(pair_free, phase.first_pair + 1 + i)
                        add_to_x(i, hidden[b % 2][:], 1.0)
                        if turn is not None or n < phase.groups - 1:
                            part(nxt, 1)
                        if turn is None and n == phase.groups - 1:
                            if stage + 1 < STAGES - 1:
                                xg_low(stage + 1, n)
                            part(nxt, 0)
                            part(nxt, 1)
                    elif kind in ("lru_in", "lru_g"):
                        for o, (side, m) in enumerate((IN_FIRST if kind == "lru_in" else IN_LAST)[n]):
                            product = (first, second)[o]
                            if side == "u":
                                nc.vector.tensor_tensor(u_ext[:, m, HALO:HALO + SEQ], product[:, 0:SEQ], rstd[:, 0:SEQ],
                                                        ALU.mult)
                                last = nc.vector.tensor_tensor(u_ext[:, m, SAMPLE + HALO:EXT - 1], product[:, SEQ:TOK],
                                                               rstd[:, SEQ:TOK], ALU.mult)
                            else:
                                last = nc.vector.tensor_tensor(gate_g[:, m, :], product, rstd[:], ALU.mult)
                        last.then_inc(pair_free, 1)
                        if kind == "lru_in":
                            taps(n - 1, 1)
                            part(nxt, 0)
                            taps(n - 1, 2)
                            part(nxt, 1)
                            taps(n - 1, 3)
                        else:
                            part(nxt, 0)
                            if n == 2:
                                y_low(0)
                            part(nxt, 1)
                            if n == 0:
                                b_square(0)
                            elif n == 1:
                                b_square(1)
                                addend()
                                for m in range(HALF):
                                    scan(m)
                            elif n == 2:
                                y_low(1)
                                y_low(2)
                                scan(HALF)
                                y_low(3)
                                scan(HALF + 1)
                                y_low(4)
                                for m in range(HALF + 2, KR):
                                    scan(m)
                            else:
                                dve.wait_ge(h_done, KR)
                                nc.vector.tensor_copy(tails[:, :, 2 * HALO:2 * HALO + 1], u_ext[:, :, SEQ - 1:SEQ]) \
                                    .then_inc(tails_done, 2)
                                nc.vector.tensor_copy(tails[:, :, 2 * HALO + 1:2 * HALO + 2], u_ext[:, :, TOK - 1:TOK]) \
                                    .then_inc(tails_done, 2)
                                for m in range(HALF, KR):
                                    y_low(m)
                    elif kind == "gates":
                        half, is_x = n // 2, n % 2
                        ms = slice(half * HALF, (half + 1) * HALF)
                        if n == 0:
                            for tap in range(1, CONV_W):
                                taps(len(IN_FIRST) - 1, tap)
                            nc.vector.tensor_copy(tails[:, :, 0:HALO], u_ext[:, :, SEQ:SEQ + HALO]).then_inc(conv_tail, 1)
                            nc.vector.tensor_copy(tails[:, :, HALO:2 * HALO], u_ext[:, :, SAMPLE + DEC:EXT - 1]) \
                                .then_inc(conv_tail, 1)
                        part(nxt, 0)
                        part(nxt, 1)
                        dve.wait_ge(gate_read, (n + 1) * HALF)
                        if is_x:
                            nc.vector.tensor_tensor(conv[:, ms, :], gated[:], conv[:, ms, :], ALU.mult) \
                                .then_inc(gated_used, 1)
                        else:
                            for m in range(half * HALF, (half + 1) * HALF):
                                s = nc.vector.tensor_scalar(rate[:, m, :], rate[:, m, :], decay[:, m:m + 1], None,
                                                            ALU.mult)
                            s.then_inc(s_done, 1)
                    elif kind == "lru_o":
                        for m in o_chunks(n):
                            add_to_x(m, bank[4 + m if n < KD // 2 else m - KD // 2][:, 0:TOK], 1.0)
                            xg_low(stage + 1, m)
                        part(nxt, 0)
                        part(nxt, 1)

                run_groups(dve, phase, step)

                if phase.name == "qkv":
                    dve.wait_ge(pair_free, phase.first_pair + phase.groups)
                    run_heads(dve, attn_step)

            inverse(STAGES - 1)
            dve.wait_ge(x_new, (STAGES - 1) * KD)
            for k in range(KD):
                nc.vector.scalar_tensor_tensor(out=y_rows[:, k, :], in0=x[:, k, :], scalar=gain[:, STAGES - 1, k:k + 1],
                                               in1=rstd[:], op0=ALU.mult, op1=ALU.mult).then_inc(out_ready, 1)

        @block.tensor
        def _(pe):
            def product(out, slot, tile, operand, k, width, start, stop):
                hi, lo = operand
                cols = slice(tile * P, (tile + 1) * P)
                nc.tensor.matmul(out, w_hi[slot][:, cols], hi[:, k, 0:width], start=start, stop=False)
                nc.tensor.matmul(out, w_hi[slot][:, cols], lo[:, k, 0:width], start=False, stop=False)
                return nc.tensor.matmul(out, w_lo[slot][:, cols], hi[:, k, 0:width], start=False, stop=stop)

            def mean(stage):
                final = stage == STAGES - 1
                pe.wait_ge(summed_squares, (stage + 1) * KD - final)
                pe.wait_ge(consts, 2)
                if final:
                    nc.tensor.matmul(bank[7][:, 0:TOK], mean_w[:], sum_squares[:], start=True, stop=False)
                    pe.wait_ge(last_squared, 1)
                    nc.tensor.matmul(bank[7][:, 0:TOK], mean_w[:], last_square[:], start=False, stop=True) \
                        .then_inc(mean_done, 1)
                    return
                nc.tensor.matmul(bank[7][:, 0:TOK], mean_w[:], sum_squares[:], start=True, stop=True) \
                    .then_inc(mean_done, 1)

            def attn_step(h, par):
                rows = slice(par * HEAD_DIM, (par + 1) * HEAD_DIM)
                if h.has(2):
                    slot = h.pair_parity(2 - par)
                    pe.wait_ge(kq_now_done, h.pair_count(2 - par, 1))
                    if not h.first(2):
                        pe.wait_ge(log_sig_done, h(1))
                    out, k, q = bank[4 + par], k_now[slot], q_now[slot]
                    for at, width, key, query in ((S0, SEQ, 0, 0), (S1, P, P, P), (C0, DEC, TOK, SEQ),
                                                  (C1, DEC, TOK + P, SEQ), (NW, DEC, SEQ, SEQ)):
                        last = nc.tensor.matmul(out[:, at:at + width], k[rows, key:key + P],
                                                q[rows, query:query + width], start=True, stop=True)
                    last.then_inc(scored, 1)
                if par == 0 and h.has(0):
                    slot = h.pair_parity(0)
                    pe.wait_ge(v_now_done, h.pair_count(0, 1))
                    if not h.first(0):
                        pe.wait_ge(v_rows_done, h.pair_count(0, 0))
                    for c in range(3):
                        last = nc.tensor.transpose(bank[0][:, c * P:(c + 1) * P], v_now[slot][:, c * P:(c + 1) * P],
                                                   ident[:])
                    last.then_inc(v_turned, 1)
                if h.has(0):
                    pe.wait_ge(stay_masked, h(1))
                    if not h.first(0):
                        pe.wait_ge(exponent_done, h(-1))
                    out, s = bank[6 + par], stay[par]
                    nc.tensor.matmul(out[:, 0:SCOLS], later[:], s[:, 0:SCOLS], start=True, stop=False)
                    nc.tensor.matmul(out[:, S0 + P:S0 + SEQ], ones[:], s[:, S1:S1 + P], start=False, stop=False)
                    nc.tensor.matmul(out[:, C0:NW], ones[:], s[:, C1:S1], start=False, stop=False)
                    nc.tensor.matmul(out[:, C0:C1], ones[:], s[:, NW:S1], start=False, stop=True) \
                        .then_inc(later_summed, 1)
                if h.turn is None and h.n == HEADS:
                    wo_early()
                if h.has(-1):
                    other = 1 - par
                    rows = slice(other * HEAD_DIM, (other + 1) * HEAD_DIM)
                    shift = -1 - other
                    slot = h.pair_parity(shift)
                    pe.wait_ge(weight_masked, h(0))
                    if other == 0:
                        pe.wait_ge(v_rows_done, h.pair_count(shift, 1))
                        if not h.first(shift, 4):
                            pe.wait_ge(o_done, h.pair_count(shift, -1))
                    out, w = bank[2 + slot], weight[other]
                    v = v_rows[slot][:].rearrange("p (c d) -> p c d", c=3)
                    old = pv_now[slot]
                    nc.tensor.matmul(out[rows, 0:SEQ], v[:, 0, rows], w[:, S0:S0 + SEQ], start=True, stop=False)
                    nc.tensor.matmul(out[rows, P:SEQ], v[:, 1, rows], w[:, S1:S1 + P], start=False, stop=True)
                    nc.tensor.matmul(out[rows, SEQ:TOK], old[:, 0, rows], w[:, C0:C1], start=True, stop=False)
                    nc.tensor.matmul(out[rows, SEQ:TOK], old[:, 1, rows], w[:, C1:NW], start=False, stop=False)
                    nc.tensor.matmul(out[rows, SEQ:TOK], v[:, 2, rows], w[:, NW:S1], start=False, stop=True) \
                        .then_inc(mixed, 1)

            def wo_early():
                pe.wait_ge(v_rows_done, PAIRS)
                for o in range(2):
                    pe.wait_ge(w_lo_done, 2 * WO.first_group + 1 + o)
                    for k in range(KD - 1):
                        pe.wait_ge(o_done, k + 1)
                        product(bank[o][:, 0:TOK], 0, o * KD + k, (o_hi, o_lo), k, TOK, k == 0, False)

            for phase in PHASES:
                stage, kind = phase.stage, phase.kind

                def step(turn, n, b, phase=phase, stage=stage, kind=kind):
                    i = index(turn, n, phase.body)
                    slot = b % 2
                    if kind == "wo" and n == 0:
                        pe.wait_ge(o_done, PAIRS)
                        for o in range(2):
                            last = product(bank[o][:, 0:TOK], 0, o * KD + KD - 1, (o_hi, o_lo), KD - 1, TOK, False, True)
                        last.then_inc(tiles_done, 1)
                        return
                    if kind == "qkv" and turn is None and n == phase.groups - 1:
                        attn_step(Head(None, -2), 0)
                        attn_step(Head(None, -1), 1)
                    parts = index(turn, 2 * (n + phase.first_group), 2 * phase.body)
                    xg = xg_of(stage)
                    if kind in ("up", "qkv", "ple", "lru_in", "lru_g"):
                        if turn is not None or n >= 2:
                            pe.wait_ge(pair_free, index(turn, n + phase.first_pair - 1, phase.body))
                        else:
                            wait(pe, pair_free, phase.first_pair - 1 + n)
                            if phase.name in ("up1", "up3"):
                                pe.wait_ge(x_new, KD * (stage - 1) + 6 + 2 * n)
                    elif kind == "down" and b % 2 == 0:
                        wait(pe, x_new, index(turn, n // 2 + KD * stage - 1, phase.body // 2))
                    elif kind == "wo":
                        if n == 1:
                            pe.wait_ge(o_done, PAIRS)
                        wait(pe, x_new, 8 * stage + 2 * (n - 1) if n >= 2 else 0)
                    elif kind == "lru_o":
                        if n == 0:
                            pe.wait_ge(gate_read, 4 * HALF)
                        if n == KD // 2:
                            pe.wait_ge(pair_free, next(p for p in PHASES if p.name == "lru_g").first_pair + len(IN_LAST))

                    pair = [bank[2 * slot][:, 0:TOK], bank[2 * slot + 1][:, 0:TOK]]
                    if kind in ("up", "qkv", "lru_in", "lru_g"):
                        outs = [(pair[o], xg, range(KD), True, True) for o in range(2)]
                    elif kind == "wo":
                        outs = [(pair[o], (o_hi, o_lo), range(KD), True, True) for o in range(2)]
                    elif kind == "down":
                        half = b % 2
                        ks = range(half * KF // 2, (half + 1) * KF // 2)
                        outs = [(bank[4 + b // 2][:, 0:TOK], (h_hi, h_lo), ks, half == 0, half == 1)]
                    elif kind == "ple":
                        layer = int(phase.name[-1])
                        outs = [(pair[1], (p_hi, p_lo), range(layer * KP, (layer + 1) * KP), True, True),
                                (pair[0], xg, range(KD), True, True)]
                    elif kind == "lru_o" and n < KD // 2:
                        half = n // 2
                        outs = [(bank[4 + n % 2 * 2 + o][:, 0:TOK], (y_hi, y_lo),
                                 range(half * HALF, (half + 1) * HALF), half == 0, half == 1) for o in range(2)]
                    elif kind == "lru_o":
                        outs = [(bank[n - KD // 2][:, 0:TOK], (y_hi, y_lo), range(KR), True, True)]
                    else:
                        outs = [(bank[(4 + n * HALF + m) % 8][:, 0:CW], (c_hi, c_lo),
                                 [n // 2 * HALF + k for k in BAND[m]], True, True) for m in range(HALF)]

                    tile = 0
                    if phase is PHASES[0] and turn is None and n == 0:
                        pe.wait_ge(first_lo_done, 1)
                    else:
                        pe.wait_ge(w_lo_done, parts + 1)
                    if n == 0 and turn is None and kind in ("up", "qkv", "lru_in"):
                        for o, ks in ((0, range(KD - 1)), (1, range(KD - 1)), (0, (KD - 1,)), (1, (KD - 1,))):
                            for k in ks:
                                if o == 0:
                                    pe.wait_ge(xg_done, KD * stage + k + 1)
                                elif k == 0:
                                    pe.wait_ge(w_lo_done, parts + 2)
                                if phase is PHASES[0] and o == 0 and k == KD // 2:
                                    pe.wait_ge(w_lo_done, 1)
                                last = product(pair[o], slot, o * KD + k, xg, k, TOK, k == 0, k == KD - 1)
                        last.then_inc(tiles_done, 1)
                        mean(stage)
                        return
                    for o, (out, operand, ks, opens, closes) in enumerate(outs):
                        if kind == "gates":
                            if n * HALF + o == 4:
                                pe.wait_ge(pair_free, next(p for p in PHASES if p.name == "lru_g").first_pair)
                            if n * HALF + o >= 8:
                                pe.wait_ge(gate_read, n * HALF + o - 7)
                        for k in ks:
                            if tile == phase.part_a:
                                pe.wait_ge(w_lo_done, parts + 2)
                            if operand is xg and n == 0 and turn is None:
                                pe.wait_ge(xg_done, 8 * stage + k + 1)
                            if kind == "down" and turn is None and n < 2:
                                pe.wait_ge(hidden_lo_done, KF * int(phase.name[-1]) + k + 1)
                            if kind == "ple" and n == 0 and turn is None and operand[0] is p_hi:
                                pe.wait_ge(p_done, 1)
                            if kind == "gates":
                                pe.wait_ge(c_done, k + 1)
                            if kind == "lru_o" and n in (0, 2) and o == 0:
                                pe.wait_ge(y_done, k + 1)
                            if kind == "ple" and n == 0 and turn is None and tile == phase.tiles - 2:
                                mean(stage)
                            last = product(out, slot, tile, operand, k, CW if kind == "gates" else TOK,
                                           opens and k == ks[0], closes and k == ks[-1])
                            tile += 1
                        if kind == "gates" and o < HALF - 1:
                            last.then_inc(gate_summed, 1)
                    last.then_inc(tiles_done, 1)

                run_groups(pe, phase, step)
                if phase.name == "qkv":
                    pe.wait_ge(attn_consts, 11)
                    run_heads(pe, attn_step)
            mean(STAGES - 1)


def next_group(phase, after, turn, n, b):
    if turn is not None or n + 2 < phase.groups:
        return phase, turn, n + 2, b + 2
    return None if after is None else (after, None, n + 2 - phase.groups, n + 2 - phase.groups)


def up_base(phase):
    return KF * int(phase.name[-1])


def taps_before(n, tap, j):
    return HALO * sum(map(len, U_OF[:n])) + (tap - 1) * len(U_OF[n]) + j


def o_chunks(n):
    return () if n < 2 else (2 * n - 4, 2 * n - 3) if n < KD // 2 else (n,)


def gate_base(phase):
    base = 0
    for p in PHASES:
        if p is phase:
            return base
        base += p.groups if p.kind in ("up", "ple") else 0


class Head:

    def __init__(self, turn, n):
        self.turn, self.n = turn, n

    def __call__(self, k):
        if self.turn is None:
            return self.n + k
        return self.turn * 4 + (self.n + k)

    def has(self, k):
        return self.turn is not None or 0 <= self.n + k < HEADS

    def first(self, k, count=2):
        return self.turn is None and self.n + k < count

    def pair(self, k):
        if self.turn is None:
            return (self.n + k) // 2
        return self.turn * 2 + (self.n + k) // 2

    def pair_count(self, k, more):
        if self.turn is None:
            return (self.n + k) // 2 + more
        return self.turn * 2 + ((self.n + k) // 2 + more)

    def pair_parity(self, k):
        return (self.n + k) // 2 % 2


def run_heads(eng, step):
    first, tail = 5, 4
    for n in range(first):
        step(Head(None, n), n % 2)
    with eng.Fori(0, (HEADS + 1 - first - tail) // 4) as turn:
        for b in range(4):
            step(Head(turn, first + b), (first + b) % 2)
    for n in range(HEADS + 1 - tail, HEADS + 1):
        step(Head(None, n), n % 2)


def tiles(w):
    return w.reshape(w.shape[0] // P, P, w.shape[1] // P, P)


def by_output(w):
    return tiles(w).transpose(2, 1, 0, 3)


def chunks(v):
    v = v.reshape(*v.shape[:-1], v.shape[-1] // P, P)
    return np.moveaxis(v, -1, 0)


def by_token(prompt, sample):
    both = np.concatenate([prompt, sample], axis=0)
    return both.reshape(both.shape[0], -1, P).transpose(2, 1, 0)


def band_tiles(blocks):
    out = []
    side = HALF * P
    for half in range(2):
        full = np.zeros((side, side), blocks.dtype)
        for n in range(LRU_BLOCKS // 2):
            at = slice(n * LRU_BLOCK, (n + 1) * LRU_BLOCK)
            full[at, at] = blocks[half * LRU_BLOCKS // 2 + n]
        cut = tiles(full)
        out.append(np.concatenate([cut[k, :, m, :] for m in range(HALF) for k in BAND[m]], axis=1))
    return out


def flat(w):
    return w.reshape(w.shape[0], P, -1)


def layout(inputs):
    get = {k: np.asarray(v) for k, v in inputs.items()}
    up, down, ple = [], [], []
    for layer in range(2):
        for n in range(2):
            g, u = by_output(get["ffn_w_gate"][layer, n]), by_output(get["ffn_w_up"][layer, n])
            up.append(flat(np.stack([g, u], axis=2)))
            d = by_output(get["ffn_w_down"][layer, n])
            d = d.reshape(KD, P, 2, KF // 2, P).transpose(0, 2, 1, 3, 4)
            down.append(flat(d.reshape(2 * KD, P, KF // 2, P)))
        gate, proj = by_output(get["ple_w_gate"][layer]), by_output(get["ple_w_proj"][layer])
        ple.append(flat(np.concatenate([proj, gate], axis=2)))

    def two_outputs(w):
        w = by_output(w)
        return flat(w.reshape(w.shape[0] // 2, 2, P, *w.shape[2:]).transpose(0, 2, 1, 3, 4))

    w_in, w_out = by_output(get["lru_w_in"][0]), by_output(get["lru_w_o"][0])

    def in_groups(groups):
        return np.stack([np.concatenate([w_in[m + (KR if side == "u" else 0)] for side, m in group], axis=1)
                         for group in groups])

    early = w_out[:KD // 2].reshape(2, 2, P, 2, HALF, P).transpose(3, 0, 2, 1, 4, 5)
    w_out_early = early.reshape(4, P, KR, P)
    band_a, band_x = band_tiles(get["lru_w_a"][0]), band_tiles(get["lru_w_x"][0])
    vecs = {
        "g": np.concatenate([get["norm_g"].reshape(8, D_MODEL), get["final_norm_g"][None]]),
        "conv_w": get["lru_conv_w"][0], "conv_b": get["lru_conv_b"][0], "b_a": get["lru_b_a"][0],
        "b_x": get["lru_b_x"][0], "lam": get["lru_lambda"][0], "h0": get["state_lru_h"][0, 0],
    }
    p = [by_token(get["p_prompt"][i, 0], get["p_sample"][i, 0]) for i in range(2)]
    past_k = get["cache_sb_k"][0, 0].reshape(PAST, PAIRS, P).transpose(2, 1, 0)
    past_v = get["cache_sb_v"][0, 0].reshape(PAST // P, P, D_MODEL).transpose(1, 0, 2)
    arrays = {
        "x": by_token(get["x_prompt"][0], get["x_sample"][0]),
        "p": np.concatenate(p, axis=1),
        "vecs": np.concatenate([chunks(vecs[n]).reshape(P, -1) for n in VECS], axis=1),
        "past_k": past_k, "past_v": past_v,
        "conv_state": chunks(get["state_lru_conv"][0, 0]).transpose(0, 2, 1),
        "up": np.concatenate(up), "down": np.concatenate(down), "ple": np.concatenate(ple),
        "qkv": two_outputs(get["sb_w_qkv"][0]), "wo": two_outputs(get["sb_w_o"][0]),
        "lru_in": flat(in_groups(IN_FIRST)), "lru_g": flat(in_groups(IN_LAST)),
        "gates": np.stack([band_a[0], band_x[0], band_a[1], band_x[1]]),
        "lru_o": flat(np.concatenate([w_out_early, w_out[KD // 2:]])),
    }
    return {k: np.ascontiguousarray(v) for k, v in arrays.items()}


_OUTS = {"y": (P, KD, TOK), "kv_new": (P, 2 * KD, TOK), "tails": (P, KR, 2 * HALO + 2)}


def kernel(**inputs):
    import concourse.bacc as _bacc
    from concourse.bass_utils import run_bass_kernel_spmd as _run

    nc = _bacc.Bacc("TRN2", target_bir_lowering=False, num_devices=1)
    arrays, aps = {}, {}
    for name, array in layout(inputs).items():
        arrays[f"in_{name}"] = array
        aps[name] = nc.dram_tensor(f"in_{name}", array.shape, mybir.dt.from_np(array.dtype), kind="ExternalInput").ap()
    for name, shape in _OUTS.items():
        aps[name] = nc.dram_tensor(f"out_{name}", shape, F32, kind="ExternalOutput").ap()
    build(nc, aps)
    r = _run(nc, [arrays], core_ids=[0]).results[0]

    y = np.asarray(r["out_y"]).transpose(2, 1, 0).reshape(TOK, D_MODEL)
    kv = np.asarray(r["out_kv_new"]).reshape(P, 2, KD, TOK).transpose(1, 3, 2, 0).reshape(2, TOK, HEADS, HEAD_DIM)
    tails = np.asarray(r["out_tails"]).transpose(2, 1, 0).reshape(2 * HALO + 2, D_RNN)
    return (y[None, :SEQ], y[None, SEQ:],
            kv[0][None, None, :SEQ], kv[1][None, None, :SEQ],
            tails[2 * HALO][None, None], tails[None, None, 0:HALO],
            kv[0][None, None, SEQ:], kv[1][None, None, SEQ:],
            tails[2 * HALO + 1][None, None], tails[None, None, HALO:2 * HALO])
```
